# Optimizing a Trainium2 kernel written in Bass

```python
import jax, jax.numpy as jnp
from jax import lax
import numpy as np

D_MODEL = 1024
BATCH = 1
SEQ = 512
DEPTH = 1

MEM_LEN = 256
ATT_HEADS = 16
ATT_KV_HEADS = 4
ATT_HEAD_DIM = 64
WINDOW = 128
HG_HEADS = 8
HG_DK = 128
HG_DV = D_MODEL // HG_HEADS
HG_CHUNK = 64
X_HEADS = 4
X_HEAD_DIM = D_MODEL // X_HEADS
N_GROUPS = 4
EXPERTS_PER_GROUP = 8
N_EXPERTS = N_GROUPS * EXPERTS_PER_GROUP
TOP_K = 2
EXPERT_FF = 512
EPS = 1e-6
NEG_BIG = -1e30
F_FLOOR = 1e-30

ATT_Q = ATT_HEADS * ATT_HEAD_DIM
ATT_KV = ATT_KV_HEADS * ATT_HEAD_DIM
HG_K = HG_HEADS * HG_DK
HG_V = HG_HEADS * HG_DV
IN_WIDTHS = (ATT_Q, ATT_KV, ATT_KV, HG_K, HG_K, HG_V, HG_V, D_MODEL, D_MODEL)
P_IN = ATT_Q + 2 * ATT_KV + 2 * HG_K + 2 * HG_V + 2 * D_MODEL

kernel_name = "hybrid_swa_sink_hgrn2_gated_merge_hier_moe"

def rms_norm(x, g):
    xf = x.astype(jnp.float32)
    y = xf * lax.rsqrt(jnp.mean(xf * xf, axis=-1, keepdims=True) + EPS)
    return (y * g.astype(jnp.float32)).astype(x.dtype)

def sliding_window_attention(q, k, v, sinks):
    B, S = q.shape[0], q.shape[1]
    nb = S // WINDOW
    G = ATT_HEADS // ATT_KV_HEADS
    f32 = jnp.float32
    qb = q.reshape(B, nb, WINDOW, ATT_KV_HEADS, G, ATT_HEAD_DIM).astype(f32)
    kb = k.reshape(B, nb, WINDOW, ATT_KV_HEADS, ATT_HEAD_DIM).astype(f32)
    vb = v.reshape(B, nb, WINDOW, ATT_KV_HEADS, ATT_HEAD_DIM).astype(f32)

    def with_prev(t):
        prev = jnp.pad(t[:, :-1], ((0, 0), (1, 0), (0, 0), (0, 0), (0, 0)))
        return jnp.concatenate([prev, t], axis=2)

    kk, vv = with_prev(kb), with_prev(vb)
    s = jnp.einsum('bnqhgd,bnshd->bnhgqs', qb, kk) * (ATT_HEAD_DIM ** -0.5)
    qi = jnp.arange(WINDOW)[:, None]
    kj = jnp.arange(2 * WINDOW)[None, :]
    dist = qi + WINDOW - kj
    blk = jnp.arange(nb)[:, None, None]
    valid = (dist >= 0) & (dist < WINDOW) & ((blk > 0) | (kj >= WINDOW))
    s = jnp.where(valid[None, :, None, None], s, NEG_BIG)
    sink = sinks.astype(f32).reshape(ATT_KV_HEADS, G)[None, None, :, :, None, None]
    m = jnp.maximum(jnp.max(s, axis=-1, keepdims=True), sink)
    p = jnp.where(valid[None, :, None, None], jnp.exp(s - m), 0.0)
    denom = jnp.sum(p, axis=-1, keepdims=True) + jnp.exp(sink - m)
    o = jnp.einsum('bnhgqs,bnshd->bnqhgd', p / denom, vv)
    return o.reshape(B, S, ATT_Q)

def hgrn2_chunkwise(q, k, logf, v):
    B, S = q.shape[0], q.shape[1]
    nc = S // HG_CHUNK

    def to_chunks(t):
        return t.reshape(B, nc, HG_CHUNK, HG_HEADS, t.shape[-1]).transpose(1, 0, 3, 2, 4)

    causal = jnp.tril(jnp.ones((HG_CHUNK, HG_CHUNK), dtype=bool))

    def step(state, xs):
        qc, kc, gc, vc = xs
        b = jnp.cumsum(gc, axis=2)
        o_inter = jnp.einsum('bhtk,bhkv->bhtv', qc * jnp.exp(b), state)
        diff = b[:, :, :, None, :] - b[:, :, None, :, :]
        decay = jnp.where(causal[:, :, None], jnp.exp(jnp.minimum(diff, 0.0)), 0.0)
        a = jnp.einsum('bhtk,bhtsk,bhsk->bhts', qc, decay, kc)
        o_intra = jnp.einsum('bhts,bhsv->bhtv', a, vc)
        b_last = b[:, :, -1:, :]
        new_state = (jnp.exp(b_last[:, :, 0, :])[..., None] * state
                     + jnp.einsum('bhsk,bhsv->bhkv', kc * jnp.exp(jnp.minimum(b_last - b, 0.0)), vc))
        return new_state, o_inter + o_intra

    s0 = jnp.zeros((B, HG_HEADS, HG_DK, HG_DV), jnp.float32)
    _, o = lax.scan(step, s0, (to_chunks(q), to_chunks(k), to_chunks(logf), to_chunks(v)))
    return o.transpose(1, 0, 3, 2, 4).reshape(B, S, HG_HEADS, HG_DV)

def cross_attention(h, memn, w_q, w_kv, w_o):
    B, S = h.shape[0], h.shape[1]
    q = (h @ w_q).reshape(B, S, X_HEADS, X_HEAD_DIM)
    k, v = jnp.split(memn @ w_kv, 2, axis=-1)
    k = k.reshape(B, -1, X_HEADS, X_HEAD_DIM)
    v = v.reshape(B, -1, X_HEADS, X_HEAD_DIM)
    s = jnp.einsum('bqhd,bmhd->bhqm', q, k).astype(jnp.float32) * (X_HEAD_DIM ** -0.5)
    p = jax.nn.softmax(s, axis=-1)
    o = jnp.einsum('bhqm,bmhd->bqhd', p, v.astype(jnp.float32)).reshape(B, S, D_MODEL)
    return o.astype(h.dtype) @ w_o

def hierarchical_moe(h, w_router, b_router, w_gate_up, w_down):
    B, S, D = h.shape
    t = h.reshape(B * S, D)
    logits = (t @ w_router + b_router).astype(jnp.float32)
    g_prob = jax.nn.softmax(logits[:, :N_GROUPS], axis=-1)
    e_logits = logits[:, N_GROUPS:].reshape(-1, N_GROUPS, EXPERTS_PER_GROUP)
    g_top, g_idx = lax.top_k(g_prob, 1)
    e_in = jnp.take_along_axis(e_logits, g_idx[:, :, None], axis=1)[:, 0]
    e_top, e_idx = lax.top_k(e_in, TOP_K)
    e_w = jax.nn.softmax(e_top, axis=-1) * g_top
    eid = g_idx * EXPERTS_PER_GROUP + e_idx
    combine = jnp.sum(jax.nn.one_hot(eid, N_EXPERTS, dtype=jnp.float32) * e_w[..., None], axis=1)
    out = jnp.zeros((B * S, D), jnp.float32)
    for e in range(N_EXPERTS):
        gate, up = jnp.split(t @ w_gate_up[e], 2, axis=-1)
        y = (jax.nn.silu(gate) * up) @ w_down[e]
        out = out + combine[:, e:e + 1] * y.astype(jnp.float32)
    return out.astype(h.dtype).reshape(B, S, D)

def setup_inputs(seed: int = 0) -> dict:
    key = jax.random.key(seed)
    ks = jax.random.split(key, 20)
    n = jax.random.normal
    D = D_MODEL
    return {
        "x": n(ks[0], (BATCH, SEQ, D), jnp.float32),
        "mem": n(ks[1], (BATCH, MEM_LEN, D), jnp.float32),
        "mix_norm": 1.0 + 0.05 * n(ks[2], (DEPTH, D), jnp.float32),
        "w_in": n(ks[3], (DEPTH, D, P_IN), jnp.float32) * D ** -0.5,
        "b_in": 0.02 * n(ks[4], (DEPTH, P_IN), jnp.float32),
        "attn_sinks": 0.5 * n(ks[5], (DEPTH, ATT_HEADS), jnp.float32),
        "hg_lb_logits": 0.5 * n(ks[6], (DEPTH, HG_K), jnp.float32),
        "hg_out_norm": 1.0 + 0.05 * n(ks[7], (DEPTH, HG_DV), jnp.float32),
        "w_out": n(ks[8], (DEPTH, D, D), jnp.float32) * D ** -0.5,
        "cross_norm": 1.0 + 0.05 * n(ks[9], (DEPTH, D), jnp.float32),
        "mem_norm": 1.0 + 0.05 * n(ks[10], (D,), jnp.float32),
        "w_cq": n(ks[11], (DEPTH, D, D), jnp.float32) * D ** -0.5,
        "w_ckv": n(ks[12], (DEPTH, D, 2 * D), jnp.float32) * D ** -0.5,
        "w_co": n(ks[13], (DEPTH, D, D), jnp.float32) * D ** -0.5,
        "ffn_norm": 1.0 + 0.05 * n(ks[14], (DEPTH, D), jnp.float32),
        "w_router": n(ks[15], (DEPTH, D, N_GROUPS + N_EXPERTS), jnp.float32) * D ** -0.5,
        "b_router": 0.01 * n(ks[16], (DEPTH, N_GROUPS + N_EXPERTS), jnp.float32),
        "w_gate_up": n(ks[17], (DEPTH, N_EXPERTS, D, 2 * EXPERT_FF), jnp.float32) * D ** -0.5,
        "w_down": n(ks[18], (DEPTH, N_EXPERTS, EXPERT_FF, D), jnp.float32) * EXPERT_FF ** -0.5,
        "final_norm": 1.0 + 0.05 * n(ks[19], (D,), jnp.float32),
    }

def reference(x, mem, mix_norm, w_in, b_in, attn_sinks, hg_lb_logits, hg_out_norm, w_out,
              cross_norm, mem_norm, w_cq, w_ckv, w_co, ffn_norm, w_router, b_router,
              w_gate_up, w_down, final_norm):
    B, S = x.shape[0], x.shape[1]
    f32 = jnp.float32
    offs = [sum(IN_WIDTHS[:i + 1]) for i in range(len(IN_WIDTHS) - 1)]
    lb_soft = jax.nn.softmax(hg_lb_logits.astype(f32), axis=0)
    lb_all = jnp.cumsum(lb_soft, axis=0) - lb_soft[0]
    memn = rms_norm(mem, mem_norm)

    for l in range(DEPTH):
        h = rms_norm(x, mix_norm[l])
        proj = h @ w_in[l] + b_in[l]
        q_a, k_a, v_a, q_h, f_h, i_h, og_h, g_a, g_h = jnp.split(proj, offs, axis=-1)

        att = sliding_window_attention(
            q_a.reshape(B, S, ATT_HEADS, ATT_HEAD_DIM),
            k_a.reshape(B, S, ATT_KV_HEADS, ATT_HEAD_DIM),
            v_a.reshape(B, S, ATT_KV_HEADS, ATT_HEAD_DIM),
            attn_sinks[l])

        lb = lb_all[l].reshape(HG_HEADS, HG_DK)
        fpre = f_h.astype(f32).reshape(B, S, HG_HEADS, HG_DK)
        f_gate = lb + (1.0 - lb) * jax.nn.sigmoid(fpre)
        logf = jnp.log(jnp.maximum(f_gate, F_FLOOR))
        k_h = (1.0 - lb) * jax.nn.sigmoid(-fpre)
        qh = jax.nn.silu(q_h.astype(f32)).reshape(B, S, HG_HEADS, HG_DK)
        vh = i_h.astype(f32).reshape(B, S, HG_HEADS, HG_DV)
        o_h = hgrn2_chunkwise(qh, k_h, logf, vh)
        hg = rms_norm(o_h, hg_out_norm[l]).reshape(B, S, HG_V) * jax.nn.silu(og_h.astype(f32))

        mix = (jax.nn.sigmoid(g_a.astype(f32)) * att + jax.nn.sigmoid(g_h.astype(f32)) * hg).astype(x.dtype)
        x = x + mix @ w_out[l]

        x = x + cross_attention(rms_norm(x, cross_norm[l]), memn, w_cq[l], w_ckv[l], w_co[l])

        x = x + hierarchical_moe(rms_norm(x, ffn_norm[l]), w_router[l], b_router[l], w_gate_up[l], w_down[l])

    return rms_norm(x, final_norm)


_drawn_inputs = setup_inputs


def setup_inputs(seed=0):
    import zlib

    import numpy as np

    out = dict(_drawn_inputs(seed))
    spreads = {}
    factors = {'attn_sinks': 8.0,
     'cross_norm': 3.005,
     'mem_norm': 2.872,
     'ffn_norm': 2.717,
     'b_router': 6.891}
    for name, (base, spread) in spreads.items():
        noise = np.random.default_rng([zlib.crc32(name.encode()), seed]).standard_normal(out[name].shape)
        drawn = base * np.exp(spread * noise) if base else spread * noise
        out[name] = __import__('jax').numpy.asarray(drawn.astype(out[name].dtype))
    for name, factor in factors.items():
        out[name] = (out[name] * factor).astype(out[name].dtype)
    return out
```

```python
import numpy as np
import concourse.bass as bass
from concourse import mybir
from concourse.alu_op_type import AluOpType as ALU
from contextlib import ExitStack

F32 = mybir.dt.float32
I32 = mybir.dt.int32
U32 = mybir.dt.uint32
ACT = mybir.ActivationFunctionType
AX = mybir.AxisListType

P = 128
SEQ, D, MEM = 512, 1024, 256
NT, MT, KC = SEQ // P, MEM // P, D // P
HEADS, KVH, HD = 16, 4, 64
NJ = 8
XH, XD = 4, 256
NG, EPG, NE, FF = 4, 8, 32, 512
EPS, NEG, FLOOR, BIG = 1e-6, -1e30, 1e-30, 1e38
LN_CUT = 2.0 ** -60
ATT_SCALE, X_SCALE = HD ** -0.5, XD ** -0.5
C_QA, C_KA, C_VA, C_QH, C_FH, C_IH, C_OG, C_GA, C_GH = 0, 1024, 1280, 1536, 2560, 3584, 4608, 5632, 6656
SLOTS = 64
LEVELS = 7


class Steps:

    def __init__(self, eng, sem, turn=0, per=0):
        self.eng, self.sem, self.base, self.per, self.n = eng, sem, turn * per, per, 0

    def did(self, ins):
        self.n += 1
        ins.then_inc(self.sem, 1)

    def sync(self):
        self.eng.wait_ge(self.sem, self.base + self.n)

    def link(self, ins):
        self.did(ins)
        self.sync()

    def close(self):
        assert self.n == self.per, f"{self.n} steps in a turn, not {self.per}"


class Order:

    def __init__(self, eng):
        self.eng, self.last = eng, None

    def ended(self, sem, value):
        self.last = (sem, value)

    def wait(self):
        if self.last:
            self.eng.wait_ge(*self.last)
            self.last = None


def build_kernel(nc, x, mem, mix_norm, w_in, b_in, attn_sinks, hg_lb_logits, hg_out_norm, w_out, cross_norm,
                 mem_norm, w_cq, w_ckv, w_co, ffn_norm, w_router, b_router, w_gate_up, w_down, final_norm, out,
                 stop=None):
    with ExitStack() as whole:
        def sb(name, shape, dt=F32, ctx=whole):
            return ctx.enter_context(nc.sbuf_tensor(name, shape, dt))

        psum = [whole.enter_context(nc.psum_tensor(f"bank{i}", [P, 512], F32)) for i in range(8)]

        ident = sb("ident", [P, P])
        ones = sb("ones", [P, P])
        mean_d = sb("mean_d", [P, P])
        eps = sb("eps", [P, 1])
        tri = sb("tri", [P, P])
        slot_row = sb("slot_row", [P, SLOTS])
        pass_first = sb("pass_first", [P, NT, SEQ // SLOTS - 1])
        router_b = sb("router_b", [P, NG + NE])
        cols = sb("cols", [P, 101])
        bias_in, g_mix, g_mem, g_cross, g_ffn, lb_in, gn_hg = (
            cols[:, a:b] for a, b in ((0, 60), (60, 68), (68, 76), (76, 84), (84, 92), (92, 100), (100, 101)))
        x_rows = sb("x_rows", [P, NT, D])
        h_rows = sb("h_rows", [P, NT, D])
        mix = x_rows[:].rearrange("p t d -> p (t d)").rearrange("p (j t) -> p j t", t=SEQ)
        k_mem = h_rows[:, 0:2].rearrange("p t d -> p (t d)").rearrange("p (k t) -> p k t", t=MEM)
        v_mem = h_rows[:, 2:4]
        routing = {n: sb(n, shape, dt) for n, shape, dt in (
            ("at_slot", [P, NT, NE], F32),
            ("row_1", [P, NT], U32), ("row_2", [P, NT], U32),
            ("weight_1", [P, NT], F32), ("weight_2", [P, NT], F32), ("longest", [1, 1], I32))}

        front_scope = ExitStack()
        x_t = sb("x_t", [P, KC, SEQ], ctx=front_scope)
        h_t = sb("h_t", [P, KC, SEQ], ctx=front_scope)
        k_dup = sb("k_dup", [P, KVH, SEQ], ctx=front_scope)
        v_kv = sb("v_kv", [P, NT, KVH * HD], ctx=front_scope)
        pack = sb("pack", [P, NJ, 12], ctx=front_scope)
        i_bias = sb("i_bias", [P, D], ctx=front_scope)
        swa_mask = sb("swa_mask", [P, 2 * P], ctx=front_scope)
        level_mask = sb("level_mask", [P, LEVELS, 64], ctx=front_scope)
        chunk_keep = sb("chunk_keep", [P, SEQ], ctx=front_scope)

        setup_phase(nc, psum, locals())
        mixer_phase(nc, psum, locals())
        if stop == "mixer":
            dump(nc, mix, out)
        if stop != "mixer":
            cross_phase(nc, psum, locals())
        front_scope.close()
        if stop is None:
            expert_phase(nc, psum, locals())


def dump(nc, t, out):
    with ExitStack() as ctx:
        dumped = ctx.enter_context(nc.semaphore("dumped"))
        block = ctx.enter_context(nc.Block())

        @block.sync
        def _(sp):
            flat = out.rearrange("o s d -> (o s d)").rearrange("(k p t) -> p k t", p=P, t=SEQ)
            sp.dma_start(flat, t[:]).then_inc(dumped, 16)
            sp.wait_ge(dumped, 16)


def dense_sems(nc, ctx, tag):
    def sem(n):
        return ctx.enter_context(nc.semaphore(f"{tag}_{n}"))
    return dict(landed=[sem(f"w_landed{q}") for q in range(4)], mm=sem("block_done"), evac=sem("bank_read"))


def dense_load(sp, S, ring, src, n0, blocks):
    with sp.Fori(0, blocks // 4) as i:
        for q in range(4):
            weights = src(sp, 4 * i + q)
            sp.wait_ge(S["mm"], n0 + 4 * i + q + 1)
            sp.dma_start(ring[:, q], weights).then_inc(S["landed"][q], 16)


def dense_mm(pe, S, ring, banks, act, n0, blocks, width, rows_out=False):
    with pe.Fori(0, blocks // 4) as i:
        for q in range(4):
            pe.wait_ge(S["landed"][q], 16 * (n0 // 4) + 16 * i + 16)
            pe.wait_ge(S["evac"], n0 + 4 * i + q + 1)
            if rows_out:
                for t in range(width // P):
                    for k in range(KC):
                        mm = pe.matmul(banks[q][:, t * P:(t + 1) * P], act[:, k, t * P:(t + 1) * P], ring[:, q, k],
                                       start=(k == 0), stop=(k == KC - 1))
            else:
                for k in range(KC):
                    mm = pe.matmul(banks[q][:, 0:width], ring[:, q, k], act[:, k, 0:width],
                                   start=(k == 0), stop=(k == KC - 1))
            mm.then_inc(S["mm"], 1)


def dense_out(eng, S, n0, blocks, take):
    with eng.Fori(0, blocks // 4) as i:
        for q in range(4):
            eng.wait_ge(S["mm"], n0 + 4 * i + q + 5)
            take(4 * i + q, q).then_inc(S["evac"], 1)


def norm_sems(nc, ctx, tag):
    return {n: ctx.enter_context(nc.semaphore(f"{tag}_{n}")) for n in ("squared", "mean", "rstd0", "steps", "done", "src")}


def norm_act(act, N, src, sq, ln, r, bank, width, eps):
    act.wait_ge(N["src"], 1)
    act.activation(sq[:, :, 0:width], src, ACT.Square).then_inc(N["squared"], 1)
    act.wait_ge(N["mean"], 1)
    act.activation(ln[:, 0:width], bank[:, 0:width], ACT.Ln, bias=eps[:, 0:1]).then_inc(N["squared"], 1)
    act.wait_ge(N["squared"], 2)
    act.activation(r[:, 0:width], ln[:, 0:width], ACT.Exp, scale=-0.5).then_inc(N["rstd0"], 1)


def norm_pe(pe, N, sq, mean_d, bank, width):
    pe.wait_ge(N["squared"], 1)
    for k in range(KC):
        mm = pe.matmul(bank[:, 0:width], mean_d[:], sq[:, k, 0:width], start=(k == 0), stop=(k == KC - 1))
    mm.then_inc(N["mean"], 1)


def newton(dve, st, r, a, mean, eps):
    st.link(dve.tensor_tensor(a, r, r, ALU.mult))
    st.link(dve.scalar_tensor_tensor(a, mean, eps, a, ALU.add, ALU.mult))
    st.link(dve.tensor_scalar(a, a, -0.5, 1.5, ALU.mult, ALU.add))
    st.link(dve.tensor_tensor(r, r, a, ALU.mult))


def norm_dve(dve, N, src, dst, g, ln, r, bank, width, eps):
    dve.wait_ge(N["rstd0"], 1)
    st = Steps(dve, N["steps"])
    newton(dve, st, r[:, 0:width], ln[:, 0:width], bank[:, 0:width], eps[:, 0:1])
    for k in range(KC):
        dve.scalar_tensor_tensor(dst[:, k, 0:width], src[:, k, 0:width], g[:, k:k + 1], r[:, 0:width],
                                 ALU.mult, ALU.mult).then_inc(N["done"], 1)


def setup_phase(nc, psum, v):
    g = v
    with ExitStack() as ctx:
        def sb(name, shape, dt=F32):
            return ctx.enter_context(nc.sbuf_tensor(name, shape, dt))

        def sem(name):
            return ctx.enter_context(nc.semaphore(name))

        x_rows = sb("x_in", [P, NT, D])
        mem_rows = sb("mem_rows", [P, MT, D])
        mem_raw = sb("mem_raw", [P, KC, MEM])
        mem_t = sb("mem_t", [P, KC, MEM])
        sq = sb("sq", [P, KC, SEQ])
        ln = sb("ln", [P, SEQ])
        r = sb("r", [P, SEQ])
        ring = sb("ring", [P, 4, KC, P])
        v_bias = sb("v_bias", [P, KVH * HD])
        sinks = sb("sinks", [P, HEADS])
        small_rows = sb("small_rows", [101, P])
        lb_e = sb("lb_e", [P, NJ])
        lb = sb("lb", [P, NJ])
        g_mix, g_mem, lb_in = g["g_mix"], g["g_mem"], g["lb_in"]

        x_landed, mem_landed, small_landed = sem("x_landed"), sem("mem_landed"), sem("small_landed")
        const, cols_tr = sem("const"), sem("cols_transposed")
        tr_x, tr_mem, x_got, mem_got = sem("tr_x"), sem("tr_mem"), sem("x_got"), sem("mem_got")
        lb_exp, lb_steps, k_steps = sem("lb_exp"), sem("lb_steps"), sem("k_steps")
        S = dense_sems(nc, ctx, "kv")
        NM, NX = norm_sems(nc, ctx, "mem"), norm_sems(nc, ctx, "x")
        ident, ones, mean_d = g["ident"], g["ones"], g["mean_d"]
        x_t, h_t = g["x_t"], g["h_t"]
        n_small = 11
        block = ctx.enter_context(nc.Block())

        @block.sync
        def _(sp):
            sp.dma_start(mem_rows[:], g["mem"][0].rearrange("(n p) d -> p n d", p=P)).then_inc(mem_landed, 16)
            sp.dma_start(x_rows[:], g["x"][0].rearrange("(n p) d -> p n d", p=P)).then_inc(x_landed, 16)
            ckv = g["w_ckv"][0].rearrange("(k p) f -> p k f", p=P)
            win = g["w_in"][0].rearrange("(k p) f -> p k f", p=P)
            dense_load(sp, S, ring, lambda e, n: ckv[:, :, bass.ds(e.snap(n * P), P)], 0, 2 * KC)
            dense_load(sp, S, ring, lambda e, n: win[:, :, bass.ds(e.snap(n * P + C_KA), P)], 16, 4)

        @block.scalar
        def _(act):
            def row(a, b, t):
                return small_rows[a:b, :], t.rearrange("(k p) -> k p", p=P)
            loads = [row(0, 60, g["b_in"][0]), row(60, 68, g["mix_norm"][0]), row(68, 76, g["mem_norm"]),
                     row(76, 84, g["cross_norm"][0]), row(84, 92, g["ffn_norm"][0]),
                     row(92, 100, g["hg_lb_logits"][0]), row(100, 101, g["hg_out_norm"][0]),
                     (sinks[:], g["attn_sinks"][0].partition_broadcast(P)),
                     (v_bias[:], g["b_in"][0, C_VA:C_QH].partition_broadcast(P)),
                     (g["i_bias"][:], g["b_in"][0, C_IH:C_OG].partition_broadcast(P)),
                     (g["router_b"][:], g["b_router"][0].partition_broadcast(P))]
            assert len(loads) == n_small
            for dst, src in loads:
                act.dma_start(dst, src).then_inc(small_landed, 16)
            act.wait_ge(lb_steps, 2)
            act.activation(lb_e[:], lb_e[:], ACT.Exp).then_inc(lb_exp, 1)
            for k in range(KC):
                act.wait_ge(tr_mem, k + 1)
                act.activation(mem_raw[:, k], psum[k % 4][:, 0:MEM], ACT.Copy).then_inc(mem_got, 1)
            act.wait_ge(const, 8)
            act.wait_ge(mem_got, KC)
            act.activation(sq[:, :, 0:MEM], mem_raw[:], ACT.Square).then_inc(NM["squared"], 1)
            act.wait_ge(NM["mean"], 1)
            act.activation(ln[:, 0:MEM], psum[4][:, 0:MEM], ACT.Ln, bias=g["eps"][:, 0:1]).then_inc(NM["squared"], 1)
            act.wait_ge(NM["squared"], 2)
            act.activation(r[:, 0:MEM], ln[:, 0:MEM], ACT.Exp, scale=-0.5).then_inc(NM["rstd0"], 1)
            for k in range(KC):
                act.wait_ge(tr_x, k + 1)
                act.activation(x_t[:, k], psum[5 + k % 2][:], ACT.Copy).then_inc(x_got, 1)
            act.wait_ge(NM["done"], KC)
            act.wait_ge(x_got, KC)
            act.activation(sq[:], x_t[:], ACT.Square).then_inc(NX["squared"], 1)
            act.wait_ge(NX["mean"], 1)
            act.activation(ln[:], psum[4][:], ACT.Ln, bias=g["eps"][:, 0:1]).then_inc(NX["squared"], 1)
            act.wait_ge(NX["squared"], 2)
            act.activation(r[:], ln[:], ACT.Exp, scale=-0.5).then_inc(NX["rstd0"], 1)

        @block.gpsimd
        def _(pool):
            st = Steps(pool, const)
            for t, c in ((ident, 0.0), (ones, 1.0), (mean_d, 1.0 / D), (g["eps"], EPS), (g["tri"], 1.0),
                         (g["swa_mask"], 0.0), (g["level_mask"], 1.0), (g["chunk_keep"], 1.0)):
                st.did(pool.memset(t[:], c))
            st.sync()
            st.did(pool.affine_select(out=ident[:], in_=ident[:], compare_op=ALU.not_equal, fill=1.0, base=0,
                                      pattern=[[-1, P]], channel_multiplier=1))
            st.did(pool.affine_select(out=g["tri"][:], in_=g["tri"][:], compare_op=ALU.is_gt, fill=0.0, base=0,
                                      pattern=[[1, P]], channel_multiplier=-1))
            m = g["swa_mask"]
            st.did(pool.affine_select(out=m[:], in_=m[:], compare_op=ALU.is_ge, fill=NEG, base=P,
                                      pattern=[[-1, 2 * P]], channel_multiplier=1))
            st.sync()
            st.did(pool.affine_select(out=m[:], in_=m[:], compare_op=ALU.is_gt, fill=NEG, base=0,
                                      pattern=[[1, 2 * P]], channel_multiplier=-1))
            ck = g["chunk_keep"]
            st.did(pool.memset(ck[:, :].rearrange("p (c t) -> p c t", t=P)[:, :, 0:1], 0.0))
            st.did(pool.iota(g["slot_row"][:], [[1, SLOTS]], base=0, channel_multiplier=0,
                             allow_small_or_imprecise_dtypes=True))
            st.did(pool.iota(g["pass_first"][:], [[0, NT], [SLOTS, SEQ // SLOTS - 1]], base=SLOTS,
                             channel_multiplier=0, allow_small_or_imprecise_dtypes=True))
            for l in range(LEVELS):
                h = 64 >> l
                lm = g["level_mask"][:, l].rearrange("p (b i) -> p b i", i=h)
                st.did(pool.affine_select(out=lm, in_=lm, compare_op=ALU.is_ge, fill=0.0, base=0,
                                          pattern=[[-2 * h, 64 // h], [0, h]], channel_multiplier=1))
                st.sync()
                st.did(pool.affine_select(out=lm, in_=lm, compare_op=ALU.is_ge, fill=0.0, base=h - 1,
                                          pattern=[[2 * h, 64 // h], [0, h]], channel_multiplier=-1))

        @block.tensor
        def _(pe):
            pe.sem_inc(S["mm"], 4)
            pe.wait_ge(const, 9)
            pe.wait_ge(small_landed, 16 * n_small)
            pe.transpose(psum[7][:, 0:101], small_rows[:], ident[0:101, 0:101]).then_inc(cols_tr, 1)
            pe.wait_ge(mem_landed, 16)
            for k in range(KC):
                if k >= 4:
                    pe.wait_ge(mem_got, k - 3)
                for t in range(MT):
                    mm = pe.transpose(psum[k % 4][:, t * P:(t + 1) * P], mem_rows[:, t, k * P:(k + 1) * P], ident[:])
                mm.then_inc(tr_mem, 1)
            pe.wait_ge(x_landed, 16)
            norm_pe(pe, NM, sq, mean_d, psum[4], MEM)
            for k in range(KC):
                if k >= 2:
                    pe.wait_ge(x_got, k - 1)
                for t in range(NT):
                    mm = pe.transpose(psum[5 + k % 2][:, t * P:(t + 1) * P], x_rows[:, t, k * P:(k + 1) * P], ident[:])
                mm.then_inc(tr_x, 1)
            pe.wait_ge(NM["done"], KC)
            pe.wait_ge(mem_got, KC)
            dense_mm(pe, S, ring, psum, mem_t, 0, KC, MEM)
            norm_pe(pe, NX, sq, mean_d, psum[4], SEQ)
            dense_mm(pe, S, ring, psum, mem_t, KC, KC, MEM, rows_out=True)
            pe.wait_ge(NX["done"], KC)
            for q in range(4):
                pe.wait_ge(S["landed"][q], 16 * 5)
                pe.wait_ge(S["evac"], 16 + q + 1)
                for t in range(1 if q < 2 else NT):
                    for k in range(KC):
                        if q < 2:
                            mm = pe.matmul(psum[q][:], ring[:, q, k], h_t[:, k], start=(k == 0), stop=(k == KC - 1))
                        else:
                            mm = pe.matmul(psum[q][:, t * P:(t + 1) * P], h_t[:, k, t * P:(t + 1) * P], ring[:, q, k],
                                           start=(k == 0), stop=(k == KC - 1))
                mm.then_inc(S["mm"], 1)

        @block.vector
        def _(dve):
            dve.sem_inc(S["evac"], 4)
            st = Steps(dve, lb_steps)
            dve.wait_ge(small_landed, 16 * n_small)
            dve.wait_ge(cols_tr, 1)
            st.link(dve.tensor_copy(g["cols"][:], psum[7][:, 0:101]))
            st.did(dve.tensor_tensor(lb_e[:], lb_in[:], lb_in[:], ALU.subtract))
            dve.wait_ge(lb_exp, 1)
            st.link(dve.reciprocal(lb[:], lb_e[:]))
            st.link(dve.tensor_tensor(lb_e[:], lb_e[:], lb[:], ALU.mult))
            st.link(dve.tensor_tensor(lb[:], lb_e[:], lb_e[:], ALU.subtract))
            pk, b = g["pack"], g["bias_in"]
            for c, col in enumerate((C_FH, C_QH, C_OG, C_GA, C_GH)):
                st.did(dve.tensor_scalar(pk[:, :, c], b[:, col // P:col // P + NJ], -1.0, None, ALU.mult))
            for c, col in enumerate((C_QH, C_QA, C_OG)):
                st.did(dve.tensor_copy(pk[:, :, 5 + c], b[:, col // P:col // P + NJ]))
            st.did(dve.tensor_copy(pk[:, :, 8], lb[:]))
            st.did(dve.tensor_scalar(pk[:, :, 9], lb[:], -1.0, 1.0, ALU.mult, ALU.add))
            st.did(dve.tensor_copy(pk[:, :, 10:12], sinks[:].rearrange("p (j u) -> p j u", u=2)))
            norm_dve(dve, NM, mem_raw, mem_t, g_mem, ln, r, psum[4], MEM, g["eps"])
            dense_out(dve, S, 0, KC, lambda n, q: dve.tensor_scalar(
                g["k_mem"][:, n, :], psum[q][:, 0:MEM], 1.0, None, ALU.mult))
            norm_dve(dve, NX, x_t, h_t, g_mix, ln, r, psum[4], SEQ, g["eps"])
            dense_out(dve, S, KC, KC, lambda n, q: dve.tensor_scalar(
                g["v_mem"][:, :, bass.ds(n * P, P)], psum[q][:, 0:MEM].rearrange("p (t f) -> p t f", f=P), 1.0, None,
                ALU.mult))
            for q in range(2):
                dve.wait_ge(S["mm"], 16 + q + 5)
                for u in range(2):
                    src = slice(u * HD, (u + 1) * HD)
                    for half in range(2):
                        last = dve.tensor_scalar(g["k_dup"][half * HD:(half + 1) * HD, 2 * q + u], psum[q][src, :],
                                                 b[src, C_KA // P + q:C_KA // P + q + 1], None, ALU.add)
                last.then_inc(S["evac"], 1)
            for q in range(2, 4):
                dve.wait_ge(S["mm"], 16 + q + 5)
                c = (q - 2) * P
                dve.tensor_tensor(g["v_kv"][:, :, c:c + P], psum[q][:].rearrange("p (t f) -> p t f", f=P),
                                  v_bias[:, c:c + P].unsqueeze(1).broadcast_to([P, NT, P]), ALU.add).then_inc(S["evac"], 1)


def mixer_phase(nc, psum, g):
    h_t, ident, eps = g["h_t"], g["ident"], g["eps"]
    with ExitStack() as ctx:
        def sb(name, shape, dt=F32, c=ctx):
            return c.enter_context(nc.sbuf_tensor(name, shape, dt))

        mix = g["mix"]
        with ExitStack() as inner:
            def t2(name, shape=(P, SEQ)):
                return [sb(f"{name}{i}", list(shape), c=inner) for i in range(2)]

            def sem(name):
                return inner.enter_context(nc.semaphore(name))

            NB = 7
            ring = sb("ring7", [P, NB, KC, P], c=inner)
            now = t2("now", (P, 12))
            qh, kh, bb, qa, gg, ga = (t2(n) for n in ("qh", "kh", "bb", "qa", "gg", "ga"))
            vh = t2("vh", (P, NT, P))
            kcur, vcur = t2("kcur"), t2("vcur", (P, NT, HD))
            e = [sb(f"e{i}", [P, SEQ], c=inner) for i in range(2)]
            s = sb("s", [P, SEQ], c=inner)
            f1 = sb("f1", [P, SEQ], c=inner)
            f2 = sb("f2", [P, SEQ], c=inner)
            dd = [sb(f"dd{i}", [P, SEQ], c=inner) for i in range(4)]
            e_b = sb("e_b", [P, SEQ], c=inner)
            rr = [sb(f"rr{i}", [P, SEQ], c=inner) for i in range(4)]
            ke, qe = sb("ke", [P, SEQ], c=inner), sb("qe", [P, SEQ], c=inner)
            d_last = ke
            ke_t = sb("ke_t", [P, NT, P], c=inner)
            state = sb("state", [P, 3, P], c=inner)
            aa = sb("aa", [P, NT, P], c=inner)
            tmp = sb("tmp", [P, 2, NT, 64], c=inner)
            sc = sb("sc", [P, 2, NT, 2 * P], c=inner)
            pt = sb("pt", [P, 14, P], c=inner)
            mx, negm, rs, den = (sb(n, [P, 2, NT], c=inner) for n in ("mx", "negm", "rs", "den"))
            osq = ke
            rms, rln, tmp_att, oo = dd
            mean_v = sb("mean_v", [P, P], c=inner)

            landed = [sem(f"win_landed{i}") for i in range(NB)]
            blocks = sem("blocks_done")
            q_ready, v_ready, qa_ready, og_ready = sem("q_ready"), sem("v_ready"), sem("qa_ready"), sem("og_ready")
            e_used = sem("e_used")
            cur, cur2, exps, lns, gates, prj = (sem("now_ready"), sem("kv_now"), sem("block_exp"), sem("f_ln"),
                                                sem("f_ready"), sem("proj_steps"))
            proj_done = sem("proj_done")
            dif, exd, mul, lev, acc = sem("diffs"), sem("decays"), sem("level_ops"), sem("level_mm"), sem("level_added")
            ke_r, ke_tr, ke_ev, st_mm, st_up = (sem("ke_ready"), sem("ke_transposed"), sem("ke_rows"), sem("state_mm"),
                                                sem("state_ready"))
            qk, mxs, pex, pn, ptr, pev, pvd = (sem("scores"), sem("row_max"), sem("row_exp"), sem("probs"),
                                               sem("probs_transposed"), sem("probs_rows"), sem("att_out"))
            sinke, mst, diag, ost, om, osqd, rst, fin = (sem("sink_exp"), sem("mixer_steps"), sem("diag_mm"),
                                                         sem("hgrn_out"), sem("out_mean"), sem("out_squared"),
                                                         sem("out_rstd"), sem("mixed"))
            mv = sem("mean_v_set")
            SA, SB_, AL0, AL1, MX0, MX1 = psum[2], psum[3], psum[4], psum[5], psum[6], psum[7]
            units = [(u, n) for n in range(NT) for u in range(2)]

            def score_at(u, n):
                bank = (SA, SB_) if n < 2 else (AL0, AL1)
                c = 0 if n == 0 else P if n == 1 else (n - 2) * 2 * P
                return bank[u], c, (P if n == 0 else 2 * P)

            tiles = [(u, n, half) for u in range(2) for n in range(NT) for half in range(2) if n or half]
            tile_no = {t: i for i, t in enumerate(tiles)}

            block = inner.enter_context(nc.Block())
            cols = (C_FH, C_QH, C_IH, C_QA, C_OG, C_GA, C_GH)

            def turns(eng, turn):
                turn(0, 0, None, 0)
                with eng.Fori(0, 3) as i:
                    turn(2 * i + 1, 1, 2 * i, i)
                    turn(2 * i + 2, 0, 2 * i + 1, i + 1)
                turn(7, 1, 6, 3)
                turn(None, 0, 7, None)

            @block.sync
            def _(sp):
                win = g["w_in"][0].rearrange("(k p) f -> p k f", p=P)
                with sp.Fori(0, NJ) as j:
                    for q in range(NB):
                        src = win[:, :, bass.ds(sp.snap(cols[q] + j * P), P)]
                        if q != 3:
                            sp.wait_ge(blocks, NB * j + (4 if q == 2 else q + 1))
                        sp.dma_start(ring[:, q], src).then_inc(landed[q], 16)

            @block.tensor
            def _(pe):
                pe.sem_inc(blocks, NB)
                pe.wait_ge(mv, 1)

                def turn(t, par, m, kv):
                    mp = 1 - par
                    for q in range(NB):
                        if t is not None:
                            pe.wait_ge(landed[q], 16 * t + 16)
                            if q < 2 and not (isinstance(t, int) and t == 0):
                                pe.wait_ge(exps, 5 * t)
                            if q >= 2:
                                pe.wait_ge((exps, q_ready, v_ready, qa_ready, og_ready)[q - 2], 5 * t + 1 if q == 2 else t + 1)
                            bank = psum[q % 2]
                            for tt in range(NT if q == 2 else 1):
                                for k in range(KC):
                                    if q == 2:
                                        mm = pe.matmul(bank[:, tt * P:(tt + 1) * P], h_t[:, k, tt * P:(tt + 1) * P],
                                                       ring[:, q, k], start=(k == 0), stop=(k == KC - 1))
                                    else:
                                        mm = pe.matmul(bank[:], ring[:, q, k], h_t[:, k], start=(k == 0),
                                                       stop=(k == KC - 1))
                            mm.then_inc(blocks, 1)
                        if m is not None:
                            piece(q, m, mp)

                def level(l, m, mp):
                    pe.wait_ge(mul, 7 * m + l + 1)
                    if l in (4, 6):
                        pe.wait_ge(acc, 7 * m + l - 2)
                    h = 64 >> l
                    bank, c0 = (AL0, AL1)[l // 2 % 2], 256 * (l % 2)
                    for c in range(NT):
                        rv = rr[l % 4][:, c * P:(c + 1) * P].rearrange("p (b h) -> p b h", h=2 * h)[:, :, h:2 * h]
                        mm = pe.matmul(bank[:, c0 + c * 64:c0 + c * 64 + 64], rr[l % 4][:, c * P:(c + 1) * P], rv,
                                       start=True, stop=True)
                    mm.then_inc(lev, 1)

                def transposes(first, last):
                    for i in range(first, last):
                        u, n, half = tiles[i]
                        bank = (SA, SB_)[i // 4 % 2]
                        src = sc[:, u, n, P * half:P * half + P]
                        mm = pe.transpose(bank[:, i % 4 * P:(i % 4 + 1) * P], src, ident[:])
                    mm.then_inc(ptr, 1)

                def piece(q, m, mp):
                    if q == 0:
                        pe.wait_ge(proj_done, m + 1)
                        pe.wait_ge(cur2, m + 1)
                        pe.wait_ge(qa_ready, m + 1)
                        pe.wait_ge(fin, m + 1)
                        for u, n in units:
                            bank, c, w = score_at(u, n)
                            rows = slice(u * HD, (u + 1) * HD)
                            k0 = max(n - 1, 0) * P
                            mm = pe.matmul(bank[:, c:c + w], qa[mp][rows, n * P:(n + 1) * P], kcur[mp][rows, k0:k0 + w],
                                           start=True, stop=True)
                        mm.then_inc(qk, 1)
                        for c in range(NT):
                            cs = slice(c * P, (c + 1) * P)
                            mm = pe.matmul(MX0[:, cs], kh[mp][:, cs], qh[mp][:, cs], start=True, stop=True)
                        mm.then_inc(diag, 1)
                    if q == 2:
                        pe.wait_ge(ke_r, 2 * m + 1)
                        for c in range(NT):
                            mm = pe.transpose(MX1[:, c * P:(c + 1) * P], ke[:, c * P:(c + 1) * P], ident[:])
                        mm.then_inc(ke_tr, 1)
                        pe.wait_ge(mxs, m + 1)
                    if q == 3:
                        pe.wait_ge(pn, m + 1)
                        transposes(0, 4)
                        transposes(4, 8)
                        level(0, m, mp)
                        level(1, m, mp)
                    if q == 4:
                        pe.wait_ge(ke_ev, m + 1)
                        pe.wait_ge(ke_r, 2 * m + 2)
                        for c in range(3):
                            mm = pe.matmul(MX0[:, c * P:(c + 1) * P], ke_t[:, c], vh[mp][:, c], start=True, stop=True)
                        mm.then_inc(st_mm, 1)
                        pe.wait_ge(pev, 4 * m + 1)
                        transposes(8, 12)
                        pe.wait_ge(pev, 4 * m + 2)
                        transposes(12, 14)
                        level(2, m, mp)
                        level(3, m, mp)
                    if q == 5:
                        level(4, m, mp)
                        level(5, m, mp)
                    if q == 6:
                        level(6, m, mp)
                        pe.wait_ge(pev, 4 * m + 4)
                        for u in range(2):
                            for n in range(NT):
                                for half in ((0, 1) if n else (1,)):
                                    mm = pe.matmul(MX1[u * HD:(u + 1) * HD, n * P:(n + 1) * P],
                                                   vcur[mp][:, n - 1 + half], pt[:, tile_no[u, n, half]],
                                                   start=(half == 0 or n == 0), stop=(half == 1), skip_group_check=True)
                        mm.then_inc(pvd, 1)
                        pe.wait_ge(st_up, 3 * m + 3)
                        pe.wait_ge(acc, 7 * m + 7)
                        for c in range(NT):
                            cs = slice(c * P, (c + 1) * P)
                            mm = pe.matmul(MX0[:, cs], vh[mp][:, c], aa[:, c], start=True, stop=(c == 0))
                            if c:
                                mm = pe.matmul(MX0[:, cs], state[:, c - 1], qe[:, cs], start=False, stop=True)
                        mm.then_inc(ost, 1)
                        pe.wait_ge(osqd, 3 * m + 1)
                        pe.matmul(SA[:], mean_v[:], osq[:], start=True, stop=True).then_inc(om, 1)
                turns(pe, turn)

            @block.scalar
            def _(act):
                def turn(t, par, m, kv):
                    mp = 1 - par
                    for q in range(NB):
                        if t is not None:
                            bank = psum[q % 2]
                            if q == 0:
                                act.wait_ge(cur, t + 1)
                            if q != 2:
                                act.wait_ge(blocks, NB + NB * t + q + 1)
                            if q == 3:
                                act.activation(qa[par][:], bank[:], ACT.Identity, bias=now[par][:, 6:7]).then_inc(qa_ready, 1)
                            elif q != 2:
                                c = (0, 1, None, None, 2, 3, 4)[q]
                                if c >= 2 or not (isinstance(t, int) and t == 0):
                                    act.wait_ge(e_used, 5 * t + c - 1)
                                act.activation(e[c % 2][:], bank[:], ACT.Exp, bias=now[par][:, c:c + 1],
                                               scale=-1.0).then_inc(exps, 1)
                            if q == 0:
                                act.wait_ge(gates, t + 1)
                                act.activation(f1[:], f1[:], ACT.Ln).then_inc(lns, 1)
                                act.activation(f2[:], f2[:], ACT.Ln).then_inc(lns, 1)
                        if m is not None:
                            piece(q, m, mp)

                def decay(i, m, src):
                    act.wait_ge(dif, 8 * m + i + 1)
                    act.activation(src[:], src[:], ACT.Exp).then_inc(exd, 1)

                def piece(q, m, mp):
                    if q == 0:
                        act.wait_ge(proj_done, m + 1)
                        act.activation(e_b[:], bb[mp][:], ACT.Exp).then_inc(exd, 1)
                        decay(0, m, d_last)
                        decay(1, m, dd[0])
                    if q == 1:
                        act.wait_ge(mxs, m + 1)
                        act.activation(den[:], den[:], ACT.Exp).then_inc(sinke, 1)
                        for i, (u, n) in enumerate(units):
                            w = slice(P if n == 0 else 0, 2 * P)
                            act.activation(sc[:, u, n, w], sc[:, u, n, w], ACT.Exp, bias=negm[:, u, n:n + 1],
                                           accum_out=rs[:, u, n:n + 1]).then_inc(pex, 1)
                        decay(2, m, dd[1])
                        decay(3, m, dd[2])
                    if q == 2:
                        decay(4, m, dd[3])
                        decay(5, m, dd[0])
                    if q == 3:
                        act.wait_ge(ke_tr, m + 1)
                        act.activation(ke_t[:].rearrange("p c k -> p (c k)"), MX1[:], ACT.Copy).then_inc(ke_ev, 1)
                        decay(6, m, dd[1])
                        decay(7, m, dd[2])
                    if q in (3, 5):
                        for at in ((0, 1) if q == 3 else (2, 3)):
                            act.wait_ge(ptr, 4 * m + at + 1)
                            w = 4 if at < 3 else 2
                            act.activation(pt[:, 4 * at:4 * at + w].rearrange("p c t -> p (c t)"),
                                           (SA, SB_)[at % 2][:, 0:w * P], ACT.Copy).then_inc(pev, 1)
                    if q == 6:
                        act.wait_ge(ost, m + 1)
                        act.activation(osq[:], MX0[:], ACT.Square).then_inc(osqd, 1)
                        act.wait_ge(om, m + 1)
                        act.activation(rln[:], SA[:], ACT.Ln, bias=eps[:, 0:1]).then_inc(osqd, 1)
                        act.wait_ge(osqd, 3 * m + 2)
                        act.activation(rms[:], rln[:], ACT.Exp, scale=-0.5).then_inc(osqd, 1)
                turns(act, turn)

            PROJ, MIX = 11, 25

            @block.gpsimd
            def _(pool):
                pool.memset(mean_v[:], 1.0 / P).then_inc(mv, 1)

            @block.vector
            def _(dve):
                dve.sem_inc(fin, 1)
                order = Order(dve)

                def turn(t, par, m, kv):
                    mp = 1 - par
                    if t is not None:
                        st = Steps(dve, prj, t, PROJ)
                        if not (isinstance(t, int) and t == 0):
                            dve.wait_ge(proj_done, t)
                            dve.wait_ge(fin, t)
                        dve.tensor_scalar(now[par][:], g["pack"][:, t, :], 1.0, None, ALU.mult).then_inc(cur, 1)
                        dve.tensor_scalar(kcur[par][:], g["k_dup"][:, kv, :], 1.0, None, ALU.mult)
                        dve.tensor_scalar(vcur[par][:], g["v_kv"][:, :, bass.ds(kv * HD, HD)], 1.0, None,
                                          ALU.mult).then_inc(cur2, 1)
                        dve.wait_ge(cur, t + 1)
                    mst_ = Steps(dve, mst, m, MIX) if m is not None else None
                    for q in range(NB):
                        if t is not None:
                            proj(q, t, par, st)
                        if m is not None:
                            piece(q, m, mp, mst_)
                    if t is not None:
                        st.close()
                    if m is not None:
                        mst_.close()
                    order.last = None

                def proj(q, t, par, st):
                    bank = psum[q % 2]
                    order.wait()
                    if q == 2:
                        dve.wait_ge(blocks, NB + NB * t + q + 1)
                        dve.tensor_tensor(vh[par][:], bank[:].rearrange("p (c f) -> p c f", f=P),
                                          g["i_bias"][:, bass.ds(t * P, P)].unsqueeze(1).broadcast_to([P, NT, P]),
                                          ALU.add).then_inc(v_ready, 1)
                        order.ended(v_ready, t + 1)
                    if q in (2, 3):
                        return
                    no = (0, 1, None, None, 2, 3, 4)[q]
                    ex = e[no % 2]
                    dve.wait_ge(exps, 5 * t + no + 1)
                    first = dve.tensor_scalar(s[:], ex[:], BIG, 1.0, ALU.min, ALU.add)
                    if q == 0:
                        st.link(first)
                    else:
                        first.then_inc(e_used, 1)
                        dve.wait_ge(e_used, 5 * t + no + 1)
                    if q == 0:
                        st.link(dve.reciprocal(s[:], s[:]))
                        st.link(dve.tensor_scalar(s[:], s[:], now[par][:, 9:10], None, ALU.mult))
                        dve.scalar_tensor_tensor(kh[par][:], ex[:], BIG, s[:], ALU.min, ALU.mult).then_inc(e_used, 1)
                        st.did(dve.tensor_scalar(f1[:], s[:], now[par][:, 8:9], FLOOR, ALU.add, ALU.max))
                        st.sync()
                        st.link(dve.tensor_scalar(f2[:], f1[:], LN_CUT, 1.0 / LN_CUT, ALU.min, ALU.mult))
                        dve.tensor_scalar(f1[:], f1[:], LN_CUT, None, ALU.max).then_inc(gates, 1)
                        order.ended(gates, t + 1)
                    elif q == 1:
                        dve.wait_ge(lns, 2 * t + 2)
                        st.did(dve.tensor_tensor(f1[:], f1[:], f2[:], ALU.add))
                        st.link(dve.reciprocal(s[:], s[:]))
                        dve.scalar_tensor_tensor(qh[par][:], bank[:], now[par][:, 5:6], s[:], ALU.add,
                                                 ALU.mult).then_inc(q_ready, 1)
                        st.did(dve.tensor_tensor_scan(bb[par][:], g["chunk_keep"][:], f1[:], 0.0, ALU.mult, ALU.add))
                        order.ended(prj, st.base + st.n)
                    elif q == 4:
                        st.link(dve.reciprocal(s[:], s[:]))
                        dve.scalar_tensor_tensor(gg[par][:], bank[:], now[par][:, 7:8], s[:], ALU.add,
                                                 ALU.mult).then_inc(og_ready, 1)
                        order.ended(og_ready, t + 1)
                    elif q == 5:
                        st.did(dve.reciprocal(ga[par][:], s[:]))
                        order.ended(prj, st.base + st.n)
                    elif q == 6:
                        st.link(dve.reciprocal(s[:], s[:]))
                        dve.tensor_tensor(gg[par][:], gg[par][:], s[:], ALU.mult).then_inc(proj_done, 1)
                        order.ended(proj_done, t + 1)

                def halves(tile, h):
                    v = tile[:].rearrange("p (b i) -> p b i", i=2 * h)
                    return v[:, :, 0:h], v[:, :, h:2 * h]

                def sub(l, m, mp):
                    order.wait()
                    h = 64 >> l
                    k1, q1 = halves(bb[mp], h)
                    dk, dq = halves(dd[l % 4], h)
                    nb = SEQ // (2 * h)
                    ref = q1[:, :, 0:1].broadcast_to([P, nb, h])
                    dve.tensor_tensor(dk, ref, k1, ALU.subtract)
                    dve.tensor_tensor(dq, q1, ref, ALU.subtract).then_inc(dif, 1)
                    order.ended(dif, 8 * m + l + 2)

                def mulq(l, m, mp):
                    order.wait()
                    h = 64 >> l
                    dve.wait_ge(exd, 9 * m + l + 3)
                    if l >= 4:
                        dve.wait_ge(lev, 7 * m + l - 3)
                    dk, dq = halves(dd[l % 4], h)
                    rk, rq = halves(rr[l % 4], h)
                    kk, qq = halves(kh[mp], h)[0], halves(qh[mp], h)[1]
                    dve.tensor_tensor(rk, kk, dk, ALU.mult)
                    dve.tensor_tensor(rq, qq, dq, ALU.mult).then_inc(mul, 1)
                    order.ended(mul, 7 * m + l + 1)

                def add(l, m, mst_, n):
                    order.wait()
                    dve.wait_ge(lev, 7 * m + l + n)
                    bank = (AL0, AL1)[l // 2 % 2]
                    mst_.link(dve.tensor_tensor(
                        tmp[:, 0:n], bank[:, 0:n * 256].rearrange("p (l c t) -> p l c t", l=n, t=64),
                        g["level_mask"][:, l:l + n].unsqueeze(2).broadcast_to([P, n, NT, 64]), ALU.mult))
                    for i in range(l, l + n):
                        h = 64 >> i
                        av = aa[:].rearrange("p c (b i) -> p c b i", i=2 * h)[:, :, :, h:2 * h]
                        if i > l:
                            dve.wait_ge(acc, 7 * m + i)
                        dve.tensor_tensor(av, av, tmp[:, i - l].rearrange("p c (b i) -> p c b i", i=h),
                                          ALU.add).then_inc(acc, 1)
                    order.ended(acc, 7 * m + l + n)

                def piece(q, m, mp, k):
                    order.wait()
                    if q == 0:
                        dve.wait_ge(proj_done, m + 1)
                        bv = bb[mp][:].rearrange("p (c t) -> p c t", t=P)
                        dve.tensor_tensor(d_last[:].rearrange("p (c t) -> p c t", t=P),
                                          bv[:, :, P - 1:P].broadcast_to([P, NT, P]), bv, ALU.subtract).then_inc(dif, 1)
                        order.ended(dif, 8 * m + 1)
                        dve.wait_ge(qk, m + 1)
                        sub(0, m, mp)
                        for i, (u, n) in enumerate(units):
                            bank, c, w = score_at(u, n)
                            o = 2 * P - w
                            k.did(dve.tensor_tensor_reduce(sc[:, u, n, o:], bank[:, c:c + w], g["swa_mask"][:, o:],
                                                           ATT_SCALE, NEG, ALU.add, ALU.max, mx[:, u, n:n + 1]))
                        k.sync()
                        sink = now[mp][:, 10:12].unsqueeze(2).broadcast_to([P, 2, NT])
                        k.link(dve.tensor_tensor(mx[:], mx[:], sink, ALU.max))
                        k.did(dve.tensor_tensor(den[:], sink, mx[:], ALU.subtract))
                        dve.tensor_scalar(negm[:], mx[:], -1.0, None, ALU.mult).then_inc(mxs, 1)
                        order.ended(mxs, m + 1)
                    if q == 1:
                        dve.wait_ge(exd, 9 * m + 2)
                        dve.tensor_tensor(ke[:], kh[mp][:], d_last[:], ALU.mult).then_inc(ke_r, 1)
                        k.did(dve.tensor_tensor(qe[:], qh[mp][:], e_b[:], ALU.mult))
                        order.ended(k.sem, k.base + k.n)
                        mulq(0, m, mp)
                        sub(1, m, mp)
                        sub(2, m, mp)
                        order.wait()
                        dve.wait_ge(diag, m + 1)
                        dve.tensor_tensor(aa[:], MX0[:].rearrange("p (c t) -> p c t", t=P),
                                          ident[:].unsqueeze(1).broadcast_to([P, NT, P]), ALU.mult).then_inc(ke_r, 1)
                        dve.wait_ge(ke_r, 2 * m + 2)
                    if q == 2:
                        dve.wait_ge(pex, 8 * m + 8)
                        dve.wait_ge(sinke, m + 1)
                        k.link(dve.tensor_tensor(den[:], den[:], rs[:], ALU.add))
                        k.link(dve.reciprocal(den[:], den[:]))
                        k.did(dve.tensor_tensor(sc[:, :, 0, P:], sc[:, :, 0, P:],
                                                den[:, :, 0:1].broadcast_to([P, 2, P]), ALU.mult))
                        for u in range(2):
                            last = dve.tensor_tensor(sc[:, u, 1:], sc[:, u, 1:],
                                                     den[:, u, 1:].unsqueeze(2).broadcast_to([P, 3, 2 * P]), ALU.mult)
                        last.then_inc(pn, 1)
                        order.ended(pn, m + 1)
                        mulq(1, m, mp)
                        mulq(2, m, mp)
                        sub(3, m, mp)
                        sub(4, m, mp)
                    if q == 3:
                        mulq(3, m, mp)
                        mulq(4, m, mp)
                        sub(5, m, mp)
                        sub(6, m, mp)
                    if q == 4:
                        add(0, m, k, 2)
                        mulq(5, m, mp)
                        mulq(6, m, mp)
                    if q == 5:
                        dve.wait_ge(st_mm, m + 1)
                        for c in range(3):
                            if c == 0:
                                last = dve.tensor_copy(state[:, 0], MX0[:, 0:P])
                            else:
                                last = dve.scalar_tensor_tensor(state[:, c], state[:, c - 1],
                                                                e_b[:, c * P + P - 1:c * P + P],
                                                                MX0[:, c * P:(c + 1) * P], ALU.mult, ALU.add)
                            last.then_inc(st_up, 1)
                            dve.wait_ge(st_up, 3 * m + c + 1)
                        add(2, m, k, 2)
                    if q == 6:
                        add(4, m, k, 2)
                        add(6, m, k, 1)
                        dve.wait_ge(pvd, m + 1)
                        order.wait()
                        k.did(dve.tensor_tensor(tmp_att[:], MX1[:], ga[mp][:], ALU.mult))
                        dve.wait_ge(osqd, 3 * m + 3)
                        newton(dve, k, rms[:], rln[:], SA[:], eps[:, 0:1])
                        k.link(dve.scalar_tensor_tensor(oo[:], MX0[:], g["gn_hg"][:, 0:1], rms[:], ALU.mult, ALU.mult))
                        k.link(dve.tensor_tensor(oo[:], oo[:], gg[mp][:], ALU.mult))
                        dve.tensor_tensor(mix[:, m, :], oo[:], tmp_att[:], ALU.add).then_inc(fin, 1)
                turns(dve, turn)


def cross_phase(nc, psum, g):
    x_t, h_t, ident, eps, mix = g["x_t"], g["h_t"], g["ident"], g["eps"], g["mix"]
    k_mem, v_mem = g["k_mem"], g["v_mem"]
    R = g["routing"]
    NR = NG + NE
    with ExitStack() as ctx:
        def sb(name, shape, dt=F32):
            return ctx.enter_context(nc.sbuf_tensor(name, shape, dt))

        def sem(name):
            return ctx.enter_context(nc.semaphore(name))

        ring = sb("ring_c", [P, 4, KC, P])
        sq = sb("sq_c", [P, KC, SEQ])
        q_x = sb("q_x", [P, KC, SEQ])
        o_x = sb("o_x", [P, KC, SEQ])
        ln, r = sb("ln_c", [P, SEQ]), sb("r_c", [P, SEQ])
        sc = [sb(f"sc_c{i}", [P, NT, MEM]) for i in range(2)]
        pt = [sb(f"pt_c{i}", [P, MT, SEQ]) for i in range(2)]
        mx, rs, den = (sb(n, [P, XH, NT]) for n in ("mx_c", "rs_c", "den_c"))
        w_r = sb("w_r", [P, KC, NR])
        S = dense_sems(nc, ctx, "c")
        N = [norm_sems(nc, ctx, f"n{i}") for i in range(2)]
        w_r_landed = sem("w_r_landed")
        scores, maxed, exped, normed, turned, rows, outs, taken = (
            sem(n) for n in ("x_scores", "x_max", "x_exp", "x_probs", "x_turned", "x_rows_s", "x_out", "x_taken"))
        x_steps = sem("x_steps")
        logits_mm, rt, r_exp, counts, back, back_got, back_got_v = (
            sem(n) for n in ("logits", "route_steps", "route_exp", "places", "turned_back", "h_taken", "x_taken_back"))
        chosen, maxrow, maxrow_got = sem("chosen"), sem("places_max"), sem("longest_s")
        consts = sem("route_consts")
        lg = sb("lg", [P, NT, NR])
        gp, geq = sb("gp", [P, NT, NG]), sb("geq", [P, NT, NG])
        g1, m1, m2, t1 = (sb(n, [P, NT]) for n in ("g1", "m1", "m2", "t1"))
        e_in, eq, oh1, oh2 = (sb(n, [P, NT, EPG]) for n in ("e_in", "eq", "oh1", "oh2"))
        prod = sb("prod", [P, NT, NG, EPG])
        sel1, sel2, both = (sb(n, [P, NT, NE]) for n in ("sel1", "sel2", "both"))
        rev = sb("rev", [P, EPG])
        e_base = sb("e_base", [P, NE])
        longest_f = sb("longest_f", [P, 1])
        place1, place2 = sb("place1", [P, NT, NE]), sb("place2", [P, NT, NE])
        in_pass = sb("in_pass", [P, NT, SEQ // SLOTS - 1])
        ROUTE_EXP = (3, 25)

        block = ctx.enter_context(nc.Block())

        def cols_of(w):
            v = w[0].rearrange("(k p) f -> p k f", p=P)
            return lambda e, n: v[:, :, bass.ds(e.snap(n * P), P)]

        @block.sync
        def _(sp):
            sp.dma_start(w_r[:], g["w_router"][0].rearrange("(k p) f -> p k f", p=P)).then_inc(w_r_landed, 16)
            for i, w in enumerate((g["w_out"], g["w_cq"], g["w_co"])):
                dense_load(sp, S, ring, cols_of(w), KC * i, KC)

        @block.gpsimd
        def _(pool):
            pool.iota(rev[:], [[-1, EPG]], base=EPG, channel_multiplier=0,
                      allow_small_or_imprecise_dtypes=True).then_inc(consts, 1)
            pool.iota(e_base[:], [[SLOTS, NE]], base=0, channel_multiplier=0,
                      allow_small_or_imprecise_dtypes=True).then_inc(consts, 1)

        def head_scores(pe, h):
            if h >= 2:
                pe.wait_ge(exped, NT * (h - 1))
            for t in range(NT):
                bank = psum[2 * (h % 2) + t // 2]
                for c in range(2):
                    mm = pe.matmul(bank[:, t % 2 * MEM:(t % 2 + 1) * MEM], q_x[:, 2 * h + c, t * P:(t + 1) * P],
                                   k_mem[:, 2 * h + c], start=(c == 0), stop=(c == 1))
            mm.then_inc(scores, 1)

        @block.tensor
        def _(pe):
            pe.sem_inc(S["mm"], 4)
            dense_mm(pe, S, ring, psum, mix, 0, KC, SEQ)
            norm_pe(pe, N[0], sq, g["mean_d"], psum[4], SEQ)
            pe.wait_ge(N[0]["done"], KC)
            dense_mm(pe, S, ring, psum, h_t, KC, KC, SEQ)
            pe.wait_ge(S["evac"], 4 + 2 * KC)
            head_scores(pe, 0)
            for h in range(XH):
                if h + 1 < XH:
                    head_scores(pe, h + 1)
                pe.wait_ge(normed, h + 1)
                for m in range(MT):
                    if h:
                        pe.wait_ge(rows, MT * h - MT + m + 1)
                    for t in range(NT):
                        mm = pe.transpose(psum[4 + m][:, t * P:(t + 1) * P], sc[h % 2][:, t, m * P:(m + 1) * P],
                                          ident[:])
                    mm.then_inc(turned, 1)
                pe.wait_ge(rows, MT * (h + 1))
                for c in range(2):
                    if h:
                        pe.wait_ge(taken, 2 * h - 2 + c + 1)
                    for m in range(MT):
                        mm = pe.matmul(psum[6 + c][:], v_mem[:, m, (2 * h + c) * P:(2 * h + c + 1) * P],
                                       pt[h % 2][:, m], start=(m == 0), stop=(m == MT - 1))
                    mm.then_inc(outs, 1)
            pe.wait_ge(taken, 2 * XH)
            dense_mm(pe, S, ring, psum, o_x, 2 * KC, KC, SEQ)
            norm_pe(pe, N[1], sq, g["mean_d"], psum[4], SEQ)
            pe.wait_ge(N[1]["done"], KC)
            pe.wait_ge(w_r_landed, 16)
            for t in range(NT):
                for k in range(KC):
                    mm = pe.matmul(psum[5][:, t * NR:(t + 1) * NR], h_t[:, k, t * P:(t + 1) * P], w_r[:, k],
                                   start=(k == 0), stop=(k == KC - 1))
            mm.then_inc(logits_mm, 1)
            pe.wait_ge(S["evac"], 4 + 3 * KC)
            for half in range(2):
                for t in range(NT):
                    for i, src in enumerate((h_t, x_t)):
                        no = half * NT + t
                        if no >= 2:
                            pe.wait_ge((back_got, back_got_v)[i], no - 1)
                        for k in range(4):
                            mm = pe.transpose(psum[2 * i + no % 2][:, k * P:(k + 1) * P],
                                              src[:, 4 * half + k, t * P:(t + 1) * P], ident[:])
                        mm.then_inc(back, 1)
            pe.wait_ge(chosen, 1)
            for t in range(NT):
                for u in range(t + 1):
                    mm = pe.matmul(psum[6][:, t * NE:(t + 1) * NE], (g["tri"] if u == t else g["ones"])[:], both[:, u],
                                   start=(u == 0), stop=(u == t))
            mm.then_inc(counts, 1)
            pe.wait_ge(maxrow, 1)
            pe.transpose(psum[7][0:1, 0:P], longest_f[:], ident[:]).then_inc(maxrow_got, 1)

        @block.scalar
        def _(act):
            def norm(i, ready):
                n = N[i]
                act.wait_ge(S["evac"], ready)
                act.activation(sq[:], x_t[:], ACT.Square).then_inc(n["squared"], 1)
                act.wait_ge(n["mean"], 1)
                act.activation(ln[:], psum[4][:], ACT.Ln, bias=eps[:, 0:1]).then_inc(n["squared"], 1)
                act.wait_ge(n["squared"], 2)
                act.activation(r[:], ln[:], ACT.Exp, scale=-0.5).then_inc(n["rstd0"], 1)
            norm(0, 4 + KC)
            for h in range(XH):
                act.wait_ge(maxed, h + 1)
                if h >= 2:
                    act.wait_ge(turned, MT * (h - 1))
                for t in range(NT):
                    bank = psum[2 * (h % 2) + t // 2]
                    act.activation(sc[h % 2][:, t], bank[:, t % 2 * MEM:(t % 2 + 1) * MEM], ACT.Exp,
                                   bias=mx[:, h, t:t + 1], scale=X_SCALE,
                                   accum_out=rs[:, h, t:t + 1]).then_inc(exped, 1)
                for m in range(MT):
                    act.wait_ge(turned, MT * h + m + 1)
                    if h >= 2:
                        act.wait_ge(outs, 2 * (h - 1))
                    act.activation(pt[h % 2][:, m], psum[4 + m][:], ACT.Copy).then_inc(rows, 1)
            norm(1, 4 + 3 * KC)
            for no in range(2 * NT):
                act.wait_ge(back, 2 * no + 1)
                half, t = divmod(no, NT)
                act.activation(g["h_rows"][:, t, 512 * half:512 * half + 512], psum[no % 2][:],
                               ACT.Copy).then_inc(back_got, 1)
                if no == 2:
                    act.wait_ge(rt, ROUTE_EXP[0])
                    act.activation(gp[:], gp[:], ACT.Exp).then_inc(r_exp, 1)
                if no == 5:
                    act.wait_ge(rt, ROUTE_EXP[1])
                    act.activation(t1[:], t1[:], ACT.Exp).then_inc(r_exp, 1)

        @block.vector
        def _(dve):
            dve.sem_inc(S["evac"], 4)

            def residual(n, q):
                return dve.tensor_tensor(x_t[:, n, :], x_t[:, n, :], psum[q][:], ALU.add)
            dense_out(dve, S, 0, KC, residual)
            norm_dve(dve, N[0], x_t, h_t, g["g_cross"], ln, r, psum[4], SEQ, eps)
            dense_out(dve, S, KC, KC, lambda n, q: dve.tensor_scalar(q_x[:, n, :], psum[q][:], 1.0, None, ALU.mult))
            st = Steps(dve, x_steps)

            def maxes(h):
                dve.wait_ge(scores, h + 1)
                for b in range(2):
                    st.did(dve.tensor_reduce(mx[:, h, 2 * b:2 * b + 2],
                                             psum[2 * (h % 2) + b][:].rearrange("p (t m) -> p t m", m=MEM), AX.X, ALU.max))
                st.sync()
                dve.tensor_scalar(mx[:, h], mx[:, h], -X_SCALE, None, ALU.mult).then_inc(maxed, 1)

            maxes(0)
            for h in range(XH):
                if h + 1 < XH:
                    maxes(h + 1)
                dve.wait_ge(exped, NT * (h + 1))
                st.link(dve.reciprocal(den[:, h], rs[:, h]))
                dve.tensor_tensor(sc[h % 2][:], sc[h % 2][:], den[:, h].unsqueeze(2).broadcast_to([P, NT, MEM]),
                                  ALU.mult).then_inc(normed, 1)
                for c in range(2):
                    dve.wait_ge(outs, 2 * h + c + 1)
                    dve.tensor_copy(o_x[:, 2 * h + c], psum[6 + c][:]).then_inc(taken, 1)
            dense_out(dve, S, 2 * KC, KC, residual)
            norm_dve(dve, N[1], x_t, h_t, g["g_ffn"], ln, r, psum[4], SEQ, eps)

            k = Steps(dve, rt)
            dve.wait_ge(logits_mm, 1)
            dve.wait_ge(consts, 2)
            k.link(dve.tensor_tensor(lg[:], psum[5][:, 0:NT * NR].rearrange("p (t f) -> p t f", f=NR),
                                     g["router_b"][:].unsqueeze(1).broadcast_to([P, NT, NR]), ALU.add))
            gl = lg[:, :, 0:NG]

            def bc(t, n):
                return t[:].unsqueeze(2).broadcast_to([P, NT, n])
            k.link(dve.tensor_reduce(g1[:], gl, AX.X, ALU.max))
            k.link(dve.tensor_tensor(gp[:], gl, bc(g1, NG), ALU.subtract))
            assert k.n == ROUTE_EXP[0]
            back_no = [0]

            def take_x(n):
                for _ in range(n):
                    no = back_no[0]
                    half, t = divmod(no, NT)
                    dve.wait_ge(back, 2 * no + 2)
                    dve.tensor_copy(g["x_rows"][:, t, 512 * half:512 * half + 512], psum[2 + no % 2][:]).then_inc(
                        back_got_v, 1)
                    back_no[0] += 1
            take_x(2)
            dve.wait_ge(r_exp, 1)
            k.link(dve.tensor_reduce(g1[:], gp[:], AX.X, ALU.add))
            k.link(dve.reciprocal(g1[:], g1[:]))
            k.link(dve.tensor_tensor(gp[:], gp[:], bc(g1, NG), ALU.mult))
            k.link(dve.tensor_reduce(g1[:], gp[:], AX.X, ALU.max))

            def first_max(one, values, top, n):
                k.link(dve.tensor_tensor(one, values, bc(top, n), ALU.is_equal))
                k.link(dve.tensor_tensor(one, one, rev[:, 0:n].unsqueeze(1).broadcast_to([P, NT, n]), ALU.mult))
                k.link(dve.tensor_reduce(t1[:], one, AX.X, ALU.max))
                k.link(dve.tensor_tensor(one, one, bc(t1, n), ALU.is_equal))
            first_max(geq[:], gp[:], g1, NG)
            grp = geq[:].unsqueeze(3).broadcast_to([P, NT, NG, EPG])
            k.link(dve.tensor_tensor(prod[:], lg[:, :, NG:].rearrange("p t (g e) -> p t g e", e=EPG), grp, ALU.mult))
            k.link(dve.tensor_reduce(e_in[:], prod[:].rearrange("p t g e -> p t e g"), AX.X, ALU.add))
            k.link(dve.tensor_reduce(m1[:], e_in[:], AX.X, ALU.max))
            first_max(oh1[:], e_in[:], m1, EPG)
            k.link(dve.scalar_tensor_tensor(eq[:], oh1[:], NEG, e_in[:], ALU.mult, ALU.add))
            k.link(dve.tensor_reduce(m2[:], eq[:], AX.X, ALU.max))
            k2 = k.n
            first_max(oh2[:], eq[:], m2, EPG)
            k.link(dve.tensor_tensor(t1[:], m2[:], m1[:], ALU.subtract))
            assert k.n == ROUTE_EXP[1], k.n
            take_x(2)
            k.did(dve.tensor_tensor(sel1[:].rearrange("p t (g e) -> p t g e", e=EPG), grp,
                                    oh1[:].unsqueeze(2).broadcast_to([P, NT, NG, EPG]), ALU.mult))
            k.did(dve.tensor_tensor(sel2[:].rearrange("p t (g e) -> p t g e", e=EPG), grp,
                                    oh2[:].unsqueeze(2).broadcast_to([P, NT, NG, EPG]), ALU.mult))
            k.sync()
            dve.tensor_tensor(both[:], sel1[:], sel2[:], ALU.add).then_inc(chosen, 1)
            dve.wait_ge(chosen, 1)
            take_x(3)
            dve.wait_ge(r_exp, 2)
            k.link(dve.tensor_scalar(m1[:], t1[:], 1.0, None, ALU.add))
            k.link(dve.reciprocal(m1[:], m1[:]))
            k.did(dve.tensor_tensor(R["weight_1"][:], m1[:], g1[:], ALU.mult))
            k.link(dve.tensor_tensor(t1[:], t1[:], m1[:], ALU.mult))
            k.link(dve.tensor_tensor(R["weight_2"][:], t1[:], g1[:], ALU.mult))
            take_x(1)
            dve.wait_ge(counts, 1)
            places = psum[6][:, 0:NT * NE].rearrange("p (t e) -> p t e", e=NE)
            pr = prod[:].rearrange("p t g e -> p t (g e)")
            k.link(dve.tensor_tensor(pr, places, e_base[:].unsqueeze(1).broadcast_to([P, NT, NE]), ALU.add))
            for chosen_one, place, row in ((sel1, place1, R["row_1"]), (sel2, place2, R["row_2"])):
                k.did(dve.tensor_tensor(place[:], chosen_one[:], places, ALU.mult))
                k.link(dve.tensor_tensor(chosen_one[:], chosen_one[:], pr, ALU.mult))
                k.did(dve.tensor_reduce(m1[:], place[:], AX.X, ALU.add))
                k.link(dve.tensor_reduce(m2[:], chosen_one[:], AX.X, ALU.add))
                k.link(dve.tensor_tensor(in_pass[:], bc(m1, SEQ // SLOTS - 1), g["pass_first"][:], ALU.is_ge))
                k.link(dve.tensor_reduce(m1[:], in_pass[:], AX.X, ALU.add))
                k.link(dve.scalar_tensor_tensor(m2[:], m1[:], float((NE - 1) * SLOTS), m2[:], ALU.mult, ALU.add))
                k.link(dve.tensor_copy(row[:], m2[:]))
            far = 65536.0
            k.link(dve.scalar_tensor_tensor(pr, places, far, both[:], ALU.add, ALU.mult))
            k.link(dve.tensor_scalar(R["at_slot"][:], pr, -far, None, ALU.add))
            dve.tensor_reduce(longest_f[:], R["at_slot"][:], AX.XY, ALU.max).then_inc(maxrow, 1)
            dve.wait_ge(maxrow_got, 1)
            k.link(dve.tensor_reduce(t1[0:1, 0:1], psum[7][0:1, 0:P], AX.X, ALU.max))
            dve.tensor_copy(R["longest"][:], t1[0:1, 0:1]).then_inc(rt, 1)

    if g["stop"] == "cross":
        dump(nc, x_t, g["out"])


def expert_phase(nc, psum, g):
    x_rows, h_rows, ident, eps = g["x_rows"], g["h_rows"], g["ident"], g["eps"]
    R = g["routing"]
    y_dram = nc.dram_tensor("expert_out", (NE * SEQ, D), F32, kind="Internal").ap()
    FC = FF // P
    with ExitStack() as ctx:
        def sb(name, shape, dt=F32, c=ctx):
            return c.enter_context(nc.sbuf_tensor(name, shape, dt))

        def sem(name, c=ctx):
            return c.enter_context(nc.semaphore(name))

        wgu = [sb(f"wgu{i}", [P, KC, 2 * FF]) for i in range(2)]
        wd = [sb(f"wd{i}", [P, FC, D]) for i in range(2)]
        sel = [sb(f"select{i}", [P, NT, SLOTS]) for i in range(2)]
        xg = [sb(f"xg{i}", [P, KC, SLOTS]) for i in range(2)]
        ee = [sb(f"ee{i}", [P, FC, SLOTS]) for i in range(2)]
        hh = [sb(f"hh{i}", [P, FC, SLOTS]) for i in range(2)]
        yy = [sb(f"yy{i}", [SLOTS, D]) for i in range(2)]
        at_pass = sb("at_pass", [P, NT, NE])

        def w_gu(e, half):
            v = g["w_gate_up"][0].rearrange("e (k p) f -> e p k f", p=P)
            return v[bass.ds(e, 1), :, 4 * half:4 * half + 4, :].rearrange("o p k f -> (o p) k f")

        def w_dn(e):
            return g["w_down"][0].rearrange("e (k p) f -> e p k f", p=P)[bass.ds(e, 1)].rearrange("o p k f -> (o p) k f")

        def gather(pe, q, bank):
            for k in range(KC):
                for t in range(NT):
                    mm = pe.matmul(bank[:, k * SLOTS:(k + 1) * SLOTS], h_rows[:, t, k * P:(k + 1) * P], sel[q][:, t],
                                   start=(t == 0), stop=(t == NT - 1))
            return mm

        def gate_up(pe, q, bank, ks):
            for m in range(2 * FC):
                for k in ks:
                    mm = pe.matmul(bank[:, m * SLOTS:(m + 1) * SLOTS], wgu[q][:, k, m * P:(m + 1) * P], xg[q][:, k],
                                   start=(k == 0), stop=(k == KC - 1))
            return mm

        def down(pe, q, banks):
            for n in range(2):
                for f in range(FC):
                    mm = pe.matmul(banks[n][0:SLOTS, :], hh[q][:, f], wd[q][:, f, n * 512:(n + 1) * 512],
                                   start=(f == 0), stop=(f == FC - 1))
            return mm

        with ExitStack() as inner:
            def s2(name):
                return [sem(f"{name}{i}", inner) for i in range(2)]
            gu_a, gu_b, dn = s2("gu_a_landed"), s2("gu_b_landed"), s2("down_landed")
            picked, gath, gath_got, gu_mm, ex, used, hid, dn_mm, y_got = (
                sem(n, inner) for n in ("picked", "gathered", "gathered_got", "gate_up_mm", "gate_exp", "gate_steps",
                                        "hidden", "down_mm", "y_got"))
            stored = s2("y_stored")
            block = inner.enter_context(nc.Block())
            G, U, Y = (psum[0], psum[1]), (psum[2], psum[3]), ((psum[4], psum[5]), (psum[6], psum[7]))

            @block.sync
            def _(sp):
                def load(e, q, wait):
                    a, b, d = w_gu(e, 0), w_gu(e, 1), w_dn(e)
                    if wait:
                        sp.wait_ge(gu_mm, e - 1)
                    sp.dma_start(wgu[q][:, 0:4], a).then_inc(gu_a[q], 16)
                    sp.dma_start(wgu[q][:, 4:8], b).then_inc(gu_b[q], 16)
                    if wait:
                        sp.wait_ge(dn_mm, e - 1)
                    sp.dma_start(wd[q][:], d).then_inc(dn[q], 16)
                for q in range(2):
                    load(q, q, False)
                with sp.Fori(1, NE // 2) as i:
                    for q in range(2):
                        load(2 * i + q, q, True)

            @block.tensor
            def _(pe):
                pe.wait_ge(picked, 1)
                gather(pe, 0, G[0]).then_inc(gath, 1)

                def expert(i, q, first=False, last=False):
                    e = 2 * i + q
                    pe.wait_ge(gath_got, e + 1)
                    if not first:
                        pe.wait_ge(hid, e - 1)
                    pe.wait_ge(gu_a[q], 16 * i + 16)
                    pe.wait_ge(gu_b[q], 16 * i + 16)
                    gate_up(pe, q, U[q], range(KC)).then_inc(gu_mm, 1)
                    if not last:
                        pe.wait_ge(picked, e + 2)
                        gather(pe, 1 - q, G[1 - q]).then_inc(gath, 1)
                    pe.wait_ge(hid, e + 1)
                    pe.wait_ge(dn[q], 16 * i + 16)
                    if not first:
                        pe.wait_ge(y_got, 2 * e - 2)
                    down(pe, q, Y[q]).then_inc(dn_mm, 1)

                expert(0, 0, first=True)
                expert(0, 1, first=True)
                with pe.Fori(1, NE // 2 - 1) as i:
                    for q in range(2):
                        expert(i, q)
                expert(NE // 2 - 1, 0)
                expert(NE // 2 - 1, 1, last=True)

            @block.scalar
            def _(act):
                def take(e, q, free):
                    act.wait_ge(gath, e + 1)
                    if free:
                        act.wait_ge(gu_mm, e - 1)
                    act.activation(xg[q][:].rearrange("p k s -> p (k s)"), G[q][:], ACT.Copy).then_inc(gath_got, 1)

                def expert(i, q, free=True, last=False):
                    e = 2 * i + q
                    act.wait_ge(gu_mm, e + 1)
                    if free:
                        act.wait_ge(hid, e - 1)
                    act.activation(ee[q][:].rearrange("p f s -> p (f s)"), U[q][:, 0:FC * SLOTS], ACT.Exp,
                                   scale=-1.0).then_inc(ex, 1)
                    if not last:
                        take(e + 1, 1 - q, free or q == 1)
                    act.wait_ge(dn_mm, e + 1)
                    if free:
                        act.wait_ge(stored[q], 16 * i)
                    for n in range(2):
                        act.activation(yy[q][:, n * 512:(n + 1) * 512], Y[q][n][0:SLOTS, :], ACT.Copy).then_inc(y_got, 1)
                    dst = y_dram[bass.ds(act.snap(e * SLOTS) if not isinstance(e, int) else e * SLOTS, SLOTS), :]
                    act.wait_ge(y_got, 2 * e + 2)
                    act.dma_start(dst, yy[q][:]).then_inc(stored[q], 16)
                take(0, 0, False)
                expert(0, 0, free=False)
                expert(0, 1, free=False)
                with act.Fori(1, NE // 2 - 1) as i:
                    for q in range(2):
                        expert(i, q)
                expert(NE // 2 - 1, 0)
                expert(NE // 2 - 1, 1, last=True)
                for q in range(2):
                    act.wait_ge(stored[q], 16 * (NE // 2))

            @block.vector
            def _(dve):
                def pick(e, q, free):
                    if free:
                        dve.wait_ge(gath, e - 1)
                    at = R["at_slot"][:, :, bass.ds(e, 1)].broadcast_to([P, NT, SLOTS])
                    dve.tensor_tensor(sel[q][:], g["slot_row"][:].unsqueeze(1).broadcast_to([P, NT, SLOTS]), at,
                                      ALU.is_equal).then_inc(picked, 1)

                def expert(e, q, free=True, last=False):
                    if free:
                        dve.wait_ge(dn_mm, e - 1)
                    dve.wait_ge(ex, e + 1)
                    st = Steps(dve, used, e, 3)
                    gate, up = (U[q][:, c * 256:c * 256 + 256].rearrange("p (f s) -> p f s", s=SLOTS) for c in (0, 1))
                    st.link(dve.tensor_scalar(ee[q][:], ee[q][:], BIG, 1.0, ALU.min, ALU.add))
                    st.link(dve.reciprocal(ee[q][:], ee[q][:]))
                    st.link(dve.tensor_tensor(hh[q][:], gate, ee[q][:], ALU.mult))
                    st.close()
                    dve.tensor_tensor(hh[q][:], hh[q][:], up, ALU.mult).then_inc(hid, 1)
                    if not last:
                        pick(e + 2, q, True)
                pick(0, 0, False)
                pick(1, 1, False)
                expert(0, 0, free=False)
                expert(1, 1, free=False)
                with dve.Fori(1, NE // 2 - 1) as i:
                    for q in range(2):
                        expert(2 * i + q, q)
                expert(NE - 2, 0, last=True)
                expert(NE - 1, 1, last=True)

        overflow_pass(nc, psum, g, locals())
    finish_phase(nc, psum, g, y_dram)


def overflow_pass(nc, psum, g, v):
    R = g["routing"]
    wgu, wd, sel, xg, ee, hh, yy, at_pass = (v[n][0] if n != "at_pass" else v[n] for n in (
        "wgu", "wd", "sel", "xg", "ee", "hh", "yy", "at_pass"))
    gather, gate_up, down, w_gu, w_dn, y_dram = (v[n] for n in ("gather", "gate_up", "down", "w_gu", "w_dn", "y_dram"))
    FC = FF // P
    PASSES = SEQ // SLOTS - 1
    with ExitStack() as ctx:
        landed, picked, gath, got, gu_mm, ex, used, hid, dn_mm, y_got, stored = (
            ctx.enter_context(nc.semaphore(f"over_{n}")) for n in (
                "landed", "picked", "gathered", "got", "gate_up", "exp", "steps", "hidden", "down", "y", "stored"))
        block = ctx.enter_context(nc.Block())
        G, U, Y = psum[0], psum[2], (psum[4], psum[5])

        def turns(eng, turn):
            n = eng.value_load(R["longest"][0:1, 0:1], min_val=0, max_val=SEQ - 1)
            with eng.If(n >= SLOTS):
                with eng.Fori(0, PASSES) as p:
                    with eng.Fori(0, NE) as e:
                        turn(p, e, p * NE + e)

        @block.sync
        def _(sp):
            def turn(p, e, n):
                a, b, d = w_gu(e, 0), w_gu(e, 1), w_dn(e)
                sp.wait_ge(stored, 16 * n + 16)
                sp.dma_start(wgu[:, 0:4], a).then_inc(landed, 16)
                sp.dma_start(wgu[:, 4:8], b).then_inc(landed, 16)
                sp.dma_start(wd[:], d).then_inc(landed, 16)
            turns(sp, turn)

        @block.tensor
        def _(pe):
            def turn(p, e, n):
                pe.wait_ge(picked, n + 1)
                gather(pe, 0, G).then_inc(gath, 1)
                pe.wait_ge(got, n + 1)
                pe.wait_ge(landed, 48 * n + 48)
                gate_up(pe, 0, U, range(KC)).then_inc(gu_mm, 1)
                pe.wait_ge(hid, n + 1)
                down(pe, 0, Y).then_inc(dn_mm, 1)
            turns(pe, turn)

        @block.scalar
        def _(act):
            act.sem_inc(stored, 16)

            def turn(p, e, n):
                act.wait_ge(gath, n + 1)
                act.activation(xg[:].rearrange("p k s -> p (k s)"), G[:], ACT.Copy).then_inc(got, 1)
                act.wait_ge(gu_mm, n + 1)
                act.activation(ee[:].rearrange("p f s -> p (f s)"), U[:, 0:FC * SLOTS], ACT.Exp,
                               scale=-1.0).then_inc(ex, 1)
                act.wait_ge(dn_mm, n + 1)
                for i in range(2):
                    act.activation(yy[:, i * 512:(i + 1) * 512], Y[i][0:SLOTS, :], ACT.Copy).then_inc(y_got, 1)
                dst = y_dram[bass.ds(act.snap((n + NE) * SLOTS), SLOTS), :]
                act.wait_ge(y_got, 2 * n + 2)
                act.dma_start(dst, yy[:]).then_inc(stored, 16)
                act.wait_ge(stored, 16 * n + 32)
            turns(act, turn)

        @block.vector
        def _(dve):
            def turn(p, e, n):
                st = Steps(dve, used, n, 5)
                dve.wait_ge(stored, 16 * n + 16)
                st.link(dve.tensor_scalar(at_pass[:, 0], g["slot_row"][:, 0:NE], 0.0, None, ALU.mult))
                st.link(dve.tensor_tensor(at_pass[:], R["at_slot"][:], g["pass_first"][:, :, bass.ds(p, 1)].broadcast_to(
                    [P, NT, NE]), ALU.subtract))
                dve.tensor_tensor(sel[:], g["slot_row"][:].unsqueeze(1).broadcast_to([P, NT, SLOTS]),
                                  at_pass[:, :, bass.ds(e, 1)].broadcast_to([P, NT, SLOTS]),
                                  ALU.is_equal).then_inc(picked, 1)
                gate, up = (U[:, c * 256:c * 256 + 256].rearrange("p (f s) -> p f s", s=SLOTS) for c in (0, 1))
                dve.wait_ge(ex, n + 1)
                st.link(dve.tensor_scalar(ee[:], ee[:], BIG, 1.0, ALU.min, ALU.add))
                st.link(dve.reciprocal(ee[:], ee[:]))
                st.link(dve.tensor_tensor(hh[:], gate, ee[:], ALU.mult))
                st.close()
                dve.tensor_tensor(hh[:], hh[:], up, ALU.mult).then_inc(hid, 1)
                dve.wait_ge(hid, n + 1)
            turns(dve, turn)


def finish_phase(nc, psum, g, y_dram):
    x_rows, h_rows, eps, R = g["x_rows"], g["h_rows"], g["eps"], g["routing"]
    with ExitStack() as ctx:
        def sb(name, shape, dt=F32):
            return ctx.enter_context(nc.sbuf_tensor(name, shape, dt))

        def sem(name):
            return ctx.enter_context(nc.semaphore(name))

        y1, y2 = sb("y1", [P, NT, D]), sb("y2", [P, NT, D])
        final_g = sb("final_g", [P, D])
        sqf = sb("sqf", [P, D])
        ss, lnf, rf, af = (sb(n, [P, NT]) for n in ("ss", "lnf", "rf", "af"))
        got = [sem(f"rows_back{t}") for t in range(NT)]
        g_landed, summed, sq_done, steps, done, stored = (
            sem(n) for n in ("g_landed", "summed", "sq_done", "fin_steps", "fin_done", "out_stored"))
        block = ctx.enter_context(nc.Block())

        @block.gpsimd
        def _(pool):
            def rows_of(table):
                for t in range(NT):
                    for y, row in ((y1, R["row_1"]), (y2, R["row_2"])):
                        pool.indirect_dma_start(out=y[:, t, :], out_offset=None, in_=table,
                                                in_offset=bass.IndirectOffsetOnAxis(ap=row[:, t:t + 1], axis=0)
                                                ).then_inc(got[t], 16)
            longest = pool.value_load(R["longest"][0:1, 0:1], min_val=0, max_val=SEQ - 1)
            with pool.If(longest >= SLOTS):
                rows_of(y_dram[:, :])
            with pool.Else():
                rows_of(y_dram[0:NE * SLOTS, :])

        @block.sync
        def _(sp):
            sp.dma_start(final_g[:], g["final_norm"].partition_broadcast(P)).then_inc(g_landed, 16)
            for t in range(NT):
                sp.wait_ge(done, t + 1)
                sp.dma_start(g["out"][0].rearrange("(n p) d -> n p d", p=P)[t], y2[:, t]).then_inc(stored, 16)
            sp.wait_ge(stored, 16 * NT)

        @block.vector
        def _(dve):
            k = Steps(dve, steps)
            dve.wait_ge(g_landed, 16)

            def total(t):
                dve.wait_ge(got[t], 32)
                k.did(dve.tensor_scalar(y1[:, t], y1[:, t], R["weight_1"][:, t:t + 1], None, ALU.mult))
                k.sync()
                k.link(dve.scalar_tensor_tensor(y1[:, t], y2[:, t], R["weight_2"][:, t:t + 1], y1[:, t], ALU.mult,
                                                ALU.add))
                dve.tensor_tensor(x_rows[:, t], x_rows[:, t], y1[:, t], ALU.add).then_inc(summed, 1)

            def scaled(t):
                dve.wait_ge(sq_done, 3 * t + 3)
                c = slice(t, t + 1)
                newton(dve, k, rf[:, c], af[:, c], ss[:, c], eps[:, 0:1])
                dve.scalar_tensor_tensor(y2[:, t], x_rows[:, t], rf[:, c], final_g[:], ALU.mult,
                                         ALU.mult).then_inc(done, 1)
            for t in range(NT):
                total(t)
                if t:
                    scaled(t - 1)
            scaled(NT - 1)

        @block.scalar
        def _(act):
            for t in range(NT):
                c = slice(t, t + 1)
                act.wait_ge(summed, t + 1)
                if t:
                    act.wait_ge(sq_done, 3 * t)
                act.activation(sqf[:], x_rows[:, t], ACT.Square, scale=D ** -0.5, accum_out=ss[:, c]).then_inc(sq_done, 1)
                act.wait_ge(sq_done, 3 * t + 1)
                act.activation(lnf[:, c], ss[:, c], ACT.Ln, bias=eps[:, 0:1]).then_inc(sq_done, 1)
                act.wait_ge(sq_done, 3 * t + 2)
                act.activation(rf[:, c], lnf[:, c], ACT.Exp, scale=-0.5).then_inc(sq_done, 1)


_INS = ["x", "mem", "mix_norm", "w_in", "b_in", "attn_sinks", "hg_lb_logits", "hg_out_norm", "w_out", "cross_norm",
        "mem_norm", "w_cq", "w_ckv", "w_co", "ffn_norm", "w_router", "b_router", "w_gate_up", "w_down", "final_norm"]


def kernel(**inputs):
    import concourse.bacc as bacc
    from concourse.bass_utils import run_bass_kernel_spmd
    nc = bacc.Bacc("TRN2", target_bir_lowering=False, num_devices=1)
    arrays, args = {}, []
    for name in _INS:
        a = np.ascontiguousarray(inputs[name])
        arrays[f"in_{name}"] = a
        args.append(nc.dram_tensor(f"in_{name}", a.shape, mybir.dt.from_np(a.dtype), kind="ExternalInput").ap())
    out = nc.dram_tensor("out", (1, SEQ, D), F32, kind="ExternalOutput").ap()
    build_kernel(nc, *args, out, stop=STOP)
    r = run_bass_kernel_spmd(nc, [arrays], core_ids=[0])
    return r.results[0]["out"]


STOP = None
```

```python
import numpy as np
import concourse.bass as bass
from concourse import mybir
from concourse.alu_op_type import AluOpType as ALU
from contextlib import ExitStack

F32 = mybir.dt.float32
F16 = mybir.dt.float16
F32R = mybir.dt.float32r
I32 = mybir.dt.int32
U32 = mybir.dt.uint32
ACT = mybir.ActivationFunctionType
AX = mybir.AxisListType

P = 128
SEQ, D, MEM = 512, 1024, 256
NT, MT, KC = SEQ // P, MEM // P, D // P
HEADS, KVH, HD = 16, 4, 64
NJ = 8
XH, XD = 4, 256
NG, EPG, NE, FF = 4, 8, 32, 512
EPS, NEG, FLOOR, BIG = 1e-6, -1e30, 1e-30, 1e38
LN_CUT = 2.0 ** -60
ATT_SCALE, X_SCALE = HD ** -0.5, XD ** -0.5
C_QA, C_KA, C_VA, C_QH, C_FH, C_IH, C_OG, C_GA, C_GH = 0, 1024, 1280, 1536, 2560, 3584, 4608, 5632, 6656
LN_EXP_SET = "natural_log_exp_and_others"
SLOTS = 64
NB = 7
LEVELS = 7


class Steps:

    def __init__(self, eng, sem, turn=0, per=0):
        self.eng, self.sem, self.base, self.per, self.n = eng, sem, turn * per, per, 0

    def did(self, ins):
        self.n += 1
        ins.then_inc(self.sem, 1)

    def sync(self):
        self.eng.wait_ge(self.sem, self.base + self.n)

    def link(self, ins):
        self.did(ins)
        self.sync()

    def close(self):
        assert self.n == self.per, f"{self.n} steps in a turn, not {self.per}"


class Order:

    def __init__(self, eng):
        self.eng, self.last = eng, None

    def ended(self, sem, value):
        self.last = (sem, value)

    def wait(self):
        if self.last:
            self.eng.wait_ge(*self.last)
            self.last = None


def build_kernel(nc, x, mem, mix_norm, w_in, b_in, attn_sinks, hg_lb_logits, hg_out_norm, w_out, cross_norm,
                 mem_norm, w_cq, w_ckv, w_co, ffn_norm, w_router, b_router, w_gate_up, w_down, final_norm, out):
    with ExitStack() as whole:
        def sb(name, shape, dt=F32, ctx=whole):
            return ctx.enter_context(nc.sbuf_tensor(name, shape, dt))

        psum = [whole.enter_context(nc.psum_tensor(f"bank{i}", [P, 512], F32)) for i in range(8)]

        ident = sb("ident", [P, P])
        ones = sb("ones", [P, P])
        mean_d = sb("mean_d", [P, P])
        eps = sb("eps", [P, 1])
        tri = sb("tri", [P, P])
        slot_row = sb("slot_row", [P, SLOTS])
        token_id = sb("token_id", [P, NT], F16)
        pass_first = sb("pass_first", [P, NT, SEQ // SLOTS - 1])
        router_b = sb("router_b", [P, NG + NE])
        cols = sb("cols", [P, 101])
        bias_in, g_mix, g_mem, g_cross, g_ffn, lb_in, gn_hg = (
            cols[:, a:b] for a, b in ((0, 60), (60, 68), (68, 76), (76, 84), (84, 92), (92, 100), (100, 101)))
        x_rows = sb("x_rows", [P, NT, D])
        mix = x_rows[:].rearrange("p t d -> p (t d)").rearrange("p (j t) -> p j t", t=SEQ)
        routing = {n: sb(n, shape, dt) for n, shape, dt in (
            ("at_slot", [P, NT, NE], F32),
            ("row_1", [P, NT], U32), ("row_2", [P, NT], U32),
            ("weight_1", [P, NT], F32), ("weight_2", [P, NT], F32), ("longest", [1, 1], I32))}

        wgu0 = sb("wgu0", [P, KC, 2 * FF])
        wd0 = sb("wd0", [P, FF // P, D])
        wgu0_flat, wd0_flat = (w[:].rearrange("p k f -> p (k f)") for w in (wgu0, wd0))
        ring7 = wgu0_flat[:, 0:NB * D].rearrange("p (b k f) -> p b k f", k=KC, f=P)
        i_bias = wgu0_flat[:, NB * D:NB * D + D]
        k_dup = wd0_flat[:, 0:KVH * SEQ].rearrange("p (h t) -> p h t", t=SEQ)
        v_kv = wd0_flat[:, KVH * SEQ:KVH * SEQ + NT * KVH * HD].rearrange("p (n f) -> p n f", n=NT)
        chunk_keep, state_keys = (wd0_flat[:, n:n + SEQ] for n in (3 * D, 3 * D + SEQ))
        weights_landed = {n: [whole.enter_context(nc.semaphore(f"{n}_landed{i}")) for i in range(2)]
                          for n in ("gate_up", "down")}
        h_dram = nc.dram_tensor("h_normed", (SEQ, D), F32, kind="Internal").ap()
        x_kept = nc.dram_tensor("x_kept", (P, KC, SEQ), F32, kind="Internal").ap()
        kv_kept = nc.dram_tensor("kv_kept", (P, NT, D), F32, kind="Internal").ap()

        front_scope = ExitStack()
        pack = sb("pack", [P, NJ, 12], ctx=front_scope)
        swa_mask = sb("swa_mask", [P, 2 * P], ctx=front_scope)
        level_mask = sb("level_mask", [P, LEVELS, 64], ctx=front_scope)

        h_hi, h_lo = (sb(n, [P, KC, SEQ], F32R, ctx=front_scope) for n in ("h_hi", "h_lo"))

        setup_phase(nc, psum, locals())
        mixer_phase(nc, psum, locals())
        front_scope.close()
        cross_phase(nc, psum, locals())
        expert_phase(nc, psum, locals())


def memory_views(kv):
    return kv[:, 0:2].rearrange("p t d -> p (t d)").rearrange("p (k t) -> p k t", t=MEM), kv[:, 2:4]


def dense_sems(nc, ctx, tag):
    def sem(n):
        return ctx.enter_context(nc.semaphore(f"{tag}_{n}"))
    return dict(landed=[sem(f"w_landed{q}") for q in range(4)], mm=sem("block_done"), evac=sem("bank_read"))


def dense_load(sp, S, ring, src, n0, blocks):
    with sp.Fori(0, blocks // 4) as i:
        for q in range(4):
            weights = src(sp, 4 * i + q)
            sp.wait_ge(S["mm"], n0 + 4 * i + q + 1)
            sp.dma_start(ring[:, q], weights).then_inc(S["landed"][q], 16)


def dense_mm(pe, S, ring, banks, act, n0, blocks, width, rows_out=False, ready=None):
    with pe.Fori(0, blocks // 4) as i:
        for q in range(4):
            pe.wait_ge(S["landed"][q], 16 * (n0 // 4) + 16 * i + 16)
            pe.wait_ge(S["evac"], n0 + 4 * i + q + 1)
            if rows_out:
                for t in range(width // P):
                    for k in range(KC):
                        mm = pe.matmul(banks[q][:, t * P:(t + 1) * P], act[:, k, t * P:(t + 1) * P], ring[:, q, k],
                                       start=(k == 0), stop=(k == KC - 1))
            else:
                for k in range(KC):
                    if ready and q == 0:
                        pe.wait_ge(ready, k + 1)
                    mm = pe.matmul(banks[q][:, 0:width], ring[:, q, k], act[:, k, 0:width],
                                   start=(k == 0), stop=(k == KC - 1))
            mm.then_inc(S["mm"], 1)


def dense_out(eng, S, n0, blocks, take):
    with eng.Fori(0, blocks // 4) as i:
        for q in range(4):
            eng.wait_ge(S["mm"], n0 + 4 * i + q + 5)
            take(4 * i + q, q).then_inc(S["evac"], 1)


def norm_sems(nc, ctx, tag):
    return {n: ctx.enter_context(nc.semaphore(f"{tag}_{n}")) for n in ("squared", "mean", "rstd0", "steps", "done", "src")}


def norm_act(act, N, src, sq, ln, r, bank, width, eps):
    act.wait_ge(N["src"], 1)
    act.activation(sq[:, :, 0:width], src, ACT.Square).then_inc(N["squared"], 1)
    act.wait_ge(N["mean"], 1)
    act.activation(ln[:, 0:width], bank[:, 0:width], ACT.Ln, bias=eps[:, 0:1]).then_inc(N["squared"], 1)
    act.wait_ge(N["squared"], 2)
    act.activation(r[:, 0:width], ln[:, 0:width], ACT.Exp, scale=-0.5).then_inc(N["rstd0"], 1)


def norm_pe(pe, N, sq, mean_d, bank, width):
    pe.wait_ge(N["squared"], 1)
    for k in range(KC):
        mm = pe.matmul(bank[:, 0:width], mean_d[:], sq[:, k, 0:width], start=(k == 0), stop=(k == KC - 1))
    mm.then_inc(N["mean"], 1)


def newton(dve, st, r, a, mean, eps):
    st.link(dve.tensor_tensor(a, r, r, ALU.mult))
    st.link(dve.scalar_tensor_tensor(a, mean, eps, a, ALU.add, ALU.mult))
    st.link(dve.tensor_scalar(a, a, -0.5, 1.5, ALU.mult, ALU.add))
    st.link(dve.tensor_tensor(r, r, a, ALU.mult))


def norm_dve(dve, N, src, dst, g, ln, r, bank, width, eps):
    dve.wait_ge(N["rstd0"], 1)
    st = Steps(dve, N["steps"])
    newton(dve, st, r[:, 0:width], ln[:, 0:width], bank[:, 0:width], eps[:, 0:1])
    for k in range(KC):
        dve.scalar_tensor_tensor(dst[:, k, 0:width], src[:, k, 0:width], g[:, k:k + 1], r[:, 0:width],
                                 ALU.mult, ALU.mult).then_inc(N["done"], 1)


def setup_phase(nc, psum, v):
    g = v
    with ExitStack() as ctx:
        def sb(name, shape, dt=F32):
            return ctx.enter_context(nc.sbuf_tensor(name, shape, dt))

        def sem(name):
            return ctx.enter_context(nc.semaphore(name))

        x_t = sb("x_first", [P, KC, SEQ])
        kv_rows = sb("kv_rows", [P, NT, D])
        k_mem, v_mem = memory_views(kv_rows)
        x_rows = g["x_rows"]
        mem_rows = sb("mem_rows", [P, MT, D])
        mem_raw = sb("mem_raw", [P, KC, MEM])
        mem_t = sb("mem_t", [P, KC, MEM])
        sq = sb("sq", [P, KC, SEQ])
        ln = sb("ln", [P, SEQ])
        r = sb("r", [P, SEQ])
        ring = sb("ring", [P, 4, KC, P])
        v_bias = sb("v_bias", [P, KVH * HD])
        sinks = sb("sinks", [P, HEADS])
        small_rows = sb("small_rows", [101, P])
        lb_e = sb("lb_e", [P, NJ])
        lb = sb("lb", [P, NJ])
        g_mix, g_mem, lb_in = g["g_mix"], g["g_mem"], g["lb_in"]

        x_landed, mem_landed, small_landed = sem("x_landed"), sem("mem_landed"), sem("small_landed")
        const, cols_tr = sem("const"), sem("cols_transposed")
        x_spilled, kv_spilled, h_high = sem("x_spilled"), sem("kv_spilled"), sem("h_high")
        tr_x, tr_mem, x_got, mem_got = sem("tr_x"), sem("tr_mem"), sem("x_got"), sem("mem_got")
        lb_exp, lb_steps, k_steps = sem("lb_exp"), sem("lb_steps"), sem("k_steps")
        S = dense_sems(nc, ctx, "kv")
        NM, NX = norm_sems(nc, ctx, "mem"), norm_sems(nc, ctx, "x")
        ident, ones, mean_d = g["ident"], g["ones"], g["mean_d"]
        block = ctx.enter_context(nc.Block())

        def row(a, b, t):
            return small_rows[a:b, :], t.rearrange("(k p) -> k p", p=P)
        small_loads = [row(0, 60, g["b_in"][0]), row(60, 68, g["mix_norm"][0]), row(68, 76, g["mem_norm"]),
                       row(76, 84, g["cross_norm"][0]), row(84, 92, g["ffn_norm"][0]),
                       row(92, 100, g["hg_lb_logits"][0]), row(100, 101, g["hg_out_norm"][0]),
                       (sinks[:], g["attn_sinks"][0].partition_broadcast(P)),
                       (v_bias[:], g["b_in"][0, C_VA:C_QH].partition_broadcast(P)),
                       (g["i_bias"][:], g["b_in"][0, C_IH:C_OG].partition_broadcast(P)),
                       (g["router_b"][:], g["b_router"][0].partition_broadcast(P))]
        n_small = len(small_loads)

        @block.sync
        def _(sp):
            sp.dma_start(mem_rows[:], g["mem"][0].rearrange("(n p) d -> p n d", p=P)).then_inc(mem_landed, 16)
            for dst, src in small_loads[::2]:
                sp.dma_start(dst, src).then_inc(small_landed, 16)
            sp.dma_start(x_rows[:], g["x"][0].rearrange("(n p) d -> p n d", p=P)).then_inc(x_landed, 16)
            ckv = g["w_ckv"][0].rearrange("(k p) f -> p k f", p=P)
            win = g["w_in"][0].rearrange("(k p) f -> p k f", p=P)
            sp.wait_ge(x_got, KC)
            sp.dma_start(g["x_kept"], x_t[:]).then_inc(x_spilled, 16)
            dense_load(sp, S, ring, lambda e, n: ckv[:, :, bass.ds(e.snap(n * P), P)], 0, 2 * KC)
            dense_load(sp, S, ring, lambda e, n: win[:, :, bass.ds(e.snap(n * P + C_KA), P)], 16, 4)
            sp.wait_ge(S["evac"], 4 + 2 * KC)
            sp.dma_start(g["kv_kept"], kv_rows[:]).then_inc(kv_spilled, 16)
            sp.wait_ge(x_spilled, 16)
            sp.wait_ge(kv_spilled, 16)

        @block.scalar
        def _(act):
            act.preload_act_table_set(LN_EXP_SET)
            for dst, src in small_loads[1::2]:
                act.dma_start(dst, src).then_inc(small_landed, 16)
            for k in range(KC):
                act.wait_ge(tr_mem, k + 1)
                act.activation(mem_raw[:, k], psum[k % 4][:, 0:MEM], ACT.Copy).then_inc(mem_got, 1)
            act.wait_ge(const, 8)
            act.wait_ge(mem_got, KC)
            act.activation(sq[:, :, 0:MEM], mem_raw[:], ACT.Square).then_inc(NM["squared"], 1)
            act.wait_ge(lb_steps, 2)
            act.activation(lb_e[:], lb_e[:], ACT.Exp).then_inc(lb_exp, 1)
            act.wait_ge(NM["mean"], 1)
            act.activation(ln[:, 0:MEM], psum[4][:, 0:MEM], ACT.Ln, bias=g["eps"][:, 0:1]).then_inc(NM["squared"], 1)
            act.wait_ge(NM["squared"], 2)
            act.activation(r[:, 0:MEM], ln[:, 0:MEM], ACT.Exp, scale=-0.5).then_inc(NM["rstd0"], 1)
            for k in range(KC):
                act.wait_ge(tr_x, k + 1)
                act.activation(x_t[:, k], psum[5 + k % 2][:], ACT.Copy).then_inc(x_got, 1)
            act.wait_ge(NM["done"], KC)
            act.wait_ge(x_got, KC)
            act.activation(sq[:], x_t[:], ACT.Square).then_inc(NX["squared"], 1)
            act.wait_ge(NX["mean"], 1)
            act.activation(ln[:], psum[4][:], ACT.Ln, bias=g["eps"][:, 0:1]).then_inc(NX["squared"], 1)
            act.wait_ge(NX["squared"], 2)
            act.activation(r[:], ln[:], ACT.Exp, scale=-0.5).then_inc(NX["rstd0"], 1)
            for k in range(KC):
                act.wait_ge(NX["done"], k + 1)
                act.activation(g["h_hi"][:, k], sq[:, k], ACT.Copy).then_inc(h_high, 1)

        @block.gpsimd
        def _(pool):
            st = Steps(pool, const)
            for t, c in ((ident, 0.0), (ones, 1.0), (mean_d, 1.0 / D), (g["eps"], EPS), (g["tri"], 1.0),
                         (g["swa_mask"], 0.0), (g["level_mask"], 1.0), (g["chunk_keep"], 1.0)):
                st.did(pool.memset(t[:], c))
            st.sync()
            st.did(pool.affine_select(out=ident[:], in_=ident[:], compare_op=ALU.not_equal, fill=1.0, base=0,
                                      pattern=[[-1, P]], channel_multiplier=1))
            st.did(pool.affine_select(out=g["tri"][:], in_=g["tri"][:], compare_op=ALU.is_gt, fill=0.0, base=0,
                                      pattern=[[1, P]], channel_multiplier=-1))
            m = g["swa_mask"]
            st.did(pool.affine_select(out=m[:], in_=m[:], compare_op=ALU.is_ge, fill=NEG, base=P,
                                      pattern=[[-1, 2 * P]], channel_multiplier=1))
            st.sync()
            st.did(pool.affine_select(out=m[:], in_=m[:], compare_op=ALU.is_gt, fill=NEG, base=0,
                                      pattern=[[1, 2 * P]], channel_multiplier=-1))
            ck = g["chunk_keep"]
            st.did(pool.memset(ck[:, :].rearrange("p (c t) -> p c t", t=P)[:, :, 0:1], 0.0))
            st.did(pool.iota(g["slot_row"][:], [[1, SLOTS]], base=0, channel_multiplier=0,
                             allow_small_or_imprecise_dtypes=True))
            st.did(pool.iota(g["pass_first"][:], [[0, NT], [SLOTS, SEQ // SLOTS - 1]], base=SLOTS,
                             channel_multiplier=0, allow_small_or_imprecise_dtypes=True))
            for l in range(LEVELS):
                h = 64 >> l
                lm = g["level_mask"][:, l].rearrange("p (b i) -> p b i", i=h)
                st.did(pool.affine_select(out=lm, in_=lm, compare_op=ALU.is_ge, fill=0.0, base=0,
                                          pattern=[[-2 * h, 64 // h], [0, h]], channel_multiplier=1))
                st.sync()
                st.did(pool.affine_select(out=lm, in_=lm, compare_op=ALU.is_ge, fill=0.0, base=h - 1,
                                          pattern=[[2 * h, 64 // h], [0, h]], channel_multiplier=-1))
            for k in range(KC):
                pool.wait_ge(h_high, k + 1)
                pool.tensor_tensor(g["h_lo"][:, k], sq[:, k], g["h_hi"][:, k].bitcast(F32), ALU.subtract).then_inc(const, 1)

        @block.tensor
        def _(pe):
            pe.sem_inc(S["mm"], 4)
            pe.wait_ge(const, 9)
            pe.wait_ge(mem_landed, 16)
            for k in range(KC):
                if k >= 4:
                    pe.wait_ge(mem_got, k - 3)
                for t in range(MT):
                    mm = pe.transpose(psum[k % 4][:, t * P:(t + 1) * P], mem_rows[:, t, k * P:(k + 1) * P], ident[:])
                mm.then_inc(tr_mem, 1)
            pe.wait_ge(small_landed, 16 * n_small)
            pe.transpose(psum[7][:, 0:101], small_rows[:], ident[0:101, 0:101]).then_inc(cols_tr, 1)
            pe.wait_ge(x_landed, 16)
            norm_pe(pe, NM, sq, mean_d, psum[4], MEM)
            for k in range(KC):
                if k >= 2:
                    pe.wait_ge(x_got, k - 1)
                for t in range(NT):
                    mm = pe.transpose(psum[5 + k % 2][:, t * P:(t + 1) * P], x_rows[:, t, k * P:(k + 1) * P], ident[:])
                mm.then_inc(tr_x, 1)
            pe.wait_ge(NM["done"], KC)
            pe.wait_ge(mem_got, KC)
            dense_mm(pe, S, ring, psum, mem_t, 0, KC, MEM)
            norm_pe(pe, NX, sq, mean_d, psum[4], SEQ)
            dense_mm(pe, S, ring, psum, mem_t, KC, KC, MEM, rows_out=True)
            pe.wait_ge(NX["done"], KC)
            for q in range(4):
                pe.wait_ge(S["landed"][q], 16 * 5)
                pe.wait_ge(S["evac"], 16 + q + 1)
                for t in range(1 if q < 2 else NT):
                    for k in range(KC):
                        if q < 2:
                            mm = pe.matmul(psum[q][:], ring[:, q, k], sq[:, k], start=(k == 0), stop=(k == KC - 1))
                        else:
                            mm = pe.matmul(psum[q][:, t * P:(t + 1) * P], sq[:, k, t * P:(t + 1) * P], ring[:, q, k],
                                           start=(k == 0), stop=(k == KC - 1))
                mm.then_inc(S["mm"], 1)

        @block.vector
        def _(dve):
            dve.sem_inc(S["evac"], 4)
            st = Steps(dve, lb_steps)
            dve.wait_ge(small_landed, 16 * n_small)
            dve.wait_ge(cols_tr, 1)
            st.link(dve.tensor_copy(g["cols"][:], psum[7][:, 0:101]))
            st.did(dve.tensor_tensor(lb_e[:], lb_in[:], lb_in[:], ALU.subtract))
            dve.wait_ge(lb_exp, 1)
            st.link(dve.reciprocal(lb[:], lb_e[:]))
            st.link(dve.tensor_tensor(lb_e[:], lb_e[:], lb[:], ALU.mult))
            st.link(dve.tensor_tensor(lb[:], lb_e[:], lb_e[:], ALU.subtract))
            pk, b = g["pack"], g["bias_in"]
            for c, col in enumerate((C_FH, C_QH, C_OG, C_GA, C_GH)):
                st.did(dve.tensor_scalar(pk[:, :, c], b[:, col // P:col // P + NJ], -1.0, None, ALU.mult))
            for c, col in enumerate((C_QH, C_QA, C_OG)):
                st.did(dve.tensor_copy(pk[:, :, 5 + c], b[:, col // P:col // P + NJ]))
            st.did(dve.tensor_copy(pk[:, :, 8], lb[:]))
            st.did(dve.tensor_scalar(pk[:, :, 9], lb[:], -1.0, 1.0, ALU.mult, ALU.add))
            st.did(dve.tensor_copy(pk[:, :, 10:12], sinks[:].rearrange("p (j u) -> p j u", u=2)))
            norm_dve(dve, NM, mem_raw, mem_t, g_mem, ln, r, psum[4], MEM, g["eps"])
            dense_out(dve, S, 0, KC, lambda n, q: dve.tensor_scalar(
                k_mem[:, n, :], psum[q][:, 0:MEM], 1.0, None, ALU.mult))
            norm_dve(dve, NX, x_t, sq, g_mix, ln, r, psum[4], SEQ, g["eps"])
            dense_out(dve, S, KC, KC, lambda n, q: dve.tensor_scalar(
                v_mem[:, :, bass.ds(n * P, P)], psum[q][:, 0:MEM].rearrange("p (t f) -> p t f", f=P), 1.0, None,
                ALU.mult))
            for q in range(2):
                dve.wait_ge(S["mm"], 16 + q + 5)
                for u in range(2):
                    src = slice(u * HD, (u + 1) * HD)
                    for half in range(2):
                        last = dve.tensor_scalar(g["k_dup"][half * HD:(half + 1) * HD, 2 * q + u], psum[q][src, :],
                                                 b[src, C_KA // P + q:C_KA // P + q + 1], None, ALU.add)
                last.then_inc(S["evac"], 1)
            for q in range(2, 4):
                dve.wait_ge(S["mm"], 16 + q + 5)
                c = (q - 2) * P
                dve.tensor_tensor(g["v_kv"][:, :, c:c + P], psum[q][:].rearrange("p (t f) -> p t f", f=P),
                                  v_bias[:, c:c + P].unsqueeze(1).broadcast_to([P, NT, P]), ALU.add).then_inc(S["evac"], 1)


def mixer_phase(nc, psum, g):
    ident, eps = g["ident"], g["eps"]
    with ExitStack() as ctx:
        def sb(name, shape, dt=F32, c=ctx):
            return c.enter_context(nc.sbuf_tensor(name, shape, dt))

        mix = g["mix"]
        with ExitStack() as inner:
            def t2(name, shape=(P, SEQ)):
                return [sb(f"{name}{i}", list(shape), c=inner) for i in range(2)]

            def sem(name):
                return inner.enter_context(nc.semaphore(name))

            ring = g["ring7"]
            now = t2("now", (P, 12))
            qh, kh, bb, qa, gg, ga = (t2(n) for n in ("qh", "kh", "bb", "qa", "gg", "ga"))
            vh = t2("vh", (P, NT, P))
            kcur, vcur = t2("kcur"), t2("vcur", (P, NT, HD))
            e = [sb(f"e{i}", [P, SEQ], c=inner) for i in range(2)]
            s = sb("s", [P, SEQ], c=inner)
            f1 = sb("f1", [P, SEQ], c=inner)
            f2 = sb("f2", [P, SEQ], c=inner)
            dd = [sb(f"dd{i}", [P, SEQ], c=inner) for i in range(4)]
            e_b = sb("e_b", [P, SEQ], c=inner)
            rr = [sb(f"rr{i}", [P, SEQ], c=inner) for i in range(4)]
            ke, qe = sb("ke", [P, SEQ], c=inner), sb("qe", [P, SEQ], c=inner)
            d_last = ke
            ke_t = g["state_keys"].rearrange("p (t f) -> p t f", f=P)
            state = sb("state", [P, 3, P], c=inner)
            aa = sb("aa", [P, NT, P], c=inner)
            tmp = sb("tmp", [P, 2, NT, 64], c=inner)
            sc = sb("sc", [P, 2, NT, 2 * P], c=inner)
            pt = sb("pt", [P, 14, P], c=inner)
            mx, negm, rs, den = (sb(n, [P, 2, NT], c=inner) for n in ("mx", "negm", "rs", "den"))
            osq = ke
            rms, rln, tmp_att, oo = dd
            mean_v = sb("mean_v", [P, P], c=inner)
            zero = sb("zero", [P, 1], c=inner)
            h_hi, h_lo = g["h_hi"], g["h_lo"]
            w_hi, w_lo = (sb(n, [P, 2, KC, P], F32R, c=inner) for n in ("w_hi", "w_lo"))

            landed = [sem(f"win_landed{i}") for i in range(NB)]
            blocks = sem("blocks_done")
            q_ready, v_ready, qa_ready, og_ready = sem("q_ready"), sem("v_ready"), sem("qa_ready"), sem("og_ready")
            e_used = sem("e_used")
            cur, cur2, exps, lns, gates, prj = (sem("now_ready"), sem("kv_now"), sem("block_exp"), sem("f_ln"),
                                                sem("f_ready"), sem("proj_steps"))
            proj_done = sem("proj_done")
            dif, exd, mul, lev, acc = sem("diffs"), sem("decays"), sem("level_ops"), sem("level_mm"), sem("level_added")
            ke_r, ke_tr, ke_ev, st_mm, st_up = (sem("ke_ready"), sem("ke_transposed"), sem("ke_rows"), sem("state_mm"),
                                                sem("state_ready"))
            qk, mxs, pex, pn, ptr, pev, pvd = (sem("scores"), sem("row_max"), sem("row_exp"), sem("probs"),
                                               sem("probs_transposed"), sem("probs_rows"), sem("att_out"))
            sinke, mst, diag, ost, om, osqd, rst, fin = (sem("sink_exp"), sem("mixer_steps"), sem("diag_mm"),
                                                         sem("hgrn_out"), sem("out_mean"), sem("out_squared"),
                                                         sem("out_rstd"), sem("mixed"))
            mv, zeroed, split = sem("mean_v_set"), sem("zeroed"), sem("weights_split")
            SA, SB_, AL0, AL1, MX0, MX1 = psum[2], psum[3], psum[4], psum[5], psum[6], psum[7]
            units = [(u, n) for n in range(NT) for u in range(2)]

            def score_at(u, n):
                bank = (SA, SB_) if n < 2 else (AL0, AL1)
                c = 0 if n == 0 else P if n == 1 else (n - 2) * 2 * P
                return bank[u], c, (P if n == 0 else 2 * P)

            tiles = [(u, n, half) for u in range(2) for n in range(NT) for half in range(2) if n or half]
            tile_no = {t: i for i, t in enumerate(tiles)}

            def halves(tile, h):
                v = tile[:].rearrange("p (b i) -> p b i", i=2 * h)
                return v[:, :, 0:h], v[:, :, h:2 * h]

            block = inner.enter_context(nc.Block())
            cols = (C_FH, C_QH, C_IH, C_QA, C_OG, C_GA, C_GH)

            def turns(eng, turn):
                turn(0, 0, None, 0)
                with eng.Fori(0, 3) as i:
                    turn(2 * i + 1, 1, 2 * i, i)
                    turn(2 * i + 2, 0, 2 * i + 1, i + 1)
                turn(7, 1, 6, 3)
                turn(None, 0, 7, None)

            @block.sync
            def _(sp):
                win = g["w_in"][0].rearrange("(k p) f -> p k f", p=P)
                with sp.Fori(0, NJ) as j:
                    for q in range(NB):
                        src = win[:, :, bass.ds(sp.snap(cols[q] + j * P), P)]
                        if q != 3:
                            sp.wait_ge(blocks, NB * j + (4 if q == 2 else q + 1))
                        sp.dma_start(ring[:, q], src).then_inc(landed[q], 16)

            @block.gpsimd
            def _(pool):
                pool.memset(mean_v[:], 1.0 / P).then_inc(mv, 1)
                pool.memset(zero[:], 0.0).then_inc(zeroed, 1)
                pool.wait_ge(zeroed, 1)

                def turn(t, par, m, kv):
                    for q in range(NB):
                        if t is not None:
                            split_block(t, q, par)
                        if m is not None and q in SUBS:
                            for l in SUBS[q]:
                                sub(l, m, 1 - par)

                def split_block(t, q, par):
                    n = NB * t + q
                    pool.wait_ge(landed[q], 16 * t + 16)
                    pool.wait_ge(blocks, n + NB - 1)
                    hi = w_hi[:, (par + q) % 2]
                    pool.tensor_tensor(hi, ring[:, q], zero[:, 0:1].unsqueeze(2).broadcast_to([P, KC, P]),
                                       ALU.add).then_inc(split, 1)
                    pool.wait_ge(split, 2 * n + 1)
                    pool.tensor_tensor(w_lo[:, (par + q) % 2], ring[:, q], hi.bitcast(F32),
                                       ALU.subtract).then_inc(split, 1)

                SUBS = {1: (-1, 0, 1, 2, 3), 3: (4,), 4: (5, 6)}

                def sub(l, m, mp):
                    if l < 0:
                        pool.wait_ge(proj_done, m + 1)
                        pool.wait_ge(fin, m + 1)
                        bv = bb[mp][:].rearrange("p (c t) -> p c t", t=P)
                        pool.tensor_tensor(d_last[:].rearrange("p (c t) -> p c t", t=P),
                                           bv[:, :, P - 1:P].broadcast_to([P, NT, P]), bv, ALU.subtract).then_inc(dif, 1)
                        return
                    if l >= 4:
                        pool.wait_ge(mul, 7 * m + l - 3)
                    h = 64 >> l
                    k1, q1 = halves(bb[mp], h)
                    dk, dq = halves(dd[l % 4], h)
                    nb = SEQ // (2 * h)
                    ref = q1[:, :, 0:1].broadcast_to([P, nb, h])
                    pool.tensor_tensor(dk, ref, k1, ALU.subtract)
                    pool.tensor_tensor(dq, q1, ref, ALU.subtract).then_inc(dif, 1)
                turns(pool, turn)

            @block.tensor
            def _(pe):
                pe.sem_inc(blocks, NB)
                pe.wait_ge(mv, 1)

                def turn(t, par, m, kv):
                    mp = 1 - par
                    for q in range(NB):
                        if t is not None:
                            pe.wait_ge(split, 2 * NB * t + 2 * q + 2)
                            if q < 2 and not (isinstance(t, int) and t == 0):
                                pe.wait_ge(exps, 5 * t)
                            if q >= 2:
                                pe.wait_ge((exps, q_ready, v_ready, qa_ready, og_ready)[q - 2], 5 * t + 1 if q == 2 else t + 1)
                            bank = psum[q % 2]
                            hi, lo = w_hi[:, (par + q) % 2], w_lo[:, (par + q) % 2]
                            for tt in range(NT if q == 2 else 1):
                                for k in range(KC):
                                    for i, (w, h) in enumerate(((hi, h_hi), (hi, h_lo), (lo, h_hi))):
                                        ends = dict(start=(k == 0 and i == 0), stop=(k == KC - 1 and i == 2))
                                        if q == 2:
                                            cs = slice(tt * P, (tt + 1) * P)
                                            mm = pe.matmul(bank[:, cs], h[:, k, cs], w[:, k], **ends)
                                        else:
                                            mm = pe.matmul(bank[:], w[:, k], h[:, k], **ends)
                            mm.then_inc(blocks, 1)
                        if m is not None:
                            piece(q, m, mp)

                def level(l, m, mp):
                    pe.wait_ge(mul, 7 * m + l + 1)
                    if l in (4, 6):
                        pe.wait_ge(acc, 7 * m + l - 2)
                    h = 64 >> l
                    bank, c0 = (AL0, AL1)[l // 2 % 2], 256 * (l % 2)
                    for c in range(NT):
                        rv = rr[l % 4][:, c * P:(c + 1) * P].rearrange("p (b h) -> p b h", h=2 * h)[:, :, h:2 * h]
                        mm = pe.matmul(bank[:, c0 + c * 64:c0 + c * 64 + 64], rr[l % 4][:, c * P:(c + 1) * P], rv,
                                       start=True, stop=True)
                    mm.then_inc(lev, 1)

                def transposes(first, last):
                    for i in range(first, last):
                        u, n, half = tiles[i]
                        bank = (SA, SB_)[i // 4 % 2]
                        src = sc[:, u, n, P * half:P * half + P]
                        mm = pe.transpose(bank[:, i % 4 * P:(i % 4 + 1) * P], src, ident[:])
                    mm.then_inc(ptr, 1)

                def piece(q, m, mp):
                    if q == 0:
                        pe.wait_ge(proj_done, m + 1)
                        pe.wait_ge(cur2, m + 1)
                        pe.wait_ge(qa_ready, m + 1)
                        pe.wait_ge(fin, m + 1)
                        for u, n in units:
                            bank, c, w = score_at(u, n)
                            rows = slice(u * HD, (u + 1) * HD)
                            k0 = max(n - 1, 0) * P
                            mm = pe.matmul(bank[:, c:c + w], qa[mp][rows, n * P:(n + 1) * P], kcur[mp][rows, k0:k0 + w],
                                           start=True, stop=True)
                        mm.then_inc(qk, 1)
                        for c in range(NT):
                            cs = slice(c * P, (c + 1) * P)
                            mm = pe.matmul(MX0[:, cs], kh[mp][:, cs], qh[mp][:, cs], start=True, stop=True)
                        mm.then_inc(diag, 1)
                    if q == 2:
                        pe.wait_ge(ke_r, 2 * m + 2)
                        for c in range(NT):
                            mm = pe.transpose(MX1[:, c * P:(c + 1) * P], ke[:, c * P:(c + 1) * P], ident[:])
                        mm.then_inc(ke_tr, 1)
                        pe.wait_ge(mxs, m + 1)
                    if q == 3:
                        pe.wait_ge(pn, m + 1)
                        transposes(0, 4)
                        transposes(4, 8)
                        level(0, m, mp)
                        level(1, m, mp)
                    if q == 4:
                        pe.wait_ge(ke_ev, m + 1)
                        pe.wait_ge(ke_r, 2 * m + 2)
                        for c in range(3):
                            mm = pe.matmul(MX0[:, c * P:(c + 1) * P], ke_t[:, c], vh[mp][:, c], start=True, stop=True)
                        mm.then_inc(st_mm, 1)
                        pe.wait_ge(pev, 4 * m + 1)
                        transposes(8, 12)
                        pe.wait_ge(pev, 4 * m + 2)
                        transposes(12, 14)
                        level(2, m, mp)
                        level(3, m, mp)
                    if q == 5:
                        level(4, m, mp)
                        level(5, m, mp)
                        level(6, m, mp)
                    if q == 6:
                        pe.wait_ge(pev, 4 * m + 4)
                        for u in range(2):
                            for n in range(NT):
                                for half in ((0, 1) if n else (1,)):
                                    mm = pe.matmul(MX1[u * HD:(u + 1) * HD, n * P:(n + 1) * P],
                                                   vcur[mp][:, n - 1 + half], pt[:, tile_no[u, n, half]],
                                                   start=(half == 0 or n == 0), stop=(half == 1), skip_group_check=True)
                        mm.then_inc(pvd, 1)
                        pe.wait_ge(st_up, 3 * m + 3)
                        pe.wait_ge(acc, 7 * m + 7)
                        for c in range(NT):
                            cs = slice(c * P, (c + 1) * P)
                            mm = pe.matmul(MX0[:, cs], vh[mp][:, c], aa[:, c], start=True, stop=(c == 0))
                            if c:
                                mm = pe.matmul(MX0[:, cs], state[:, c - 1], qe[:, cs], start=False, stop=True)
                        mm.then_inc(ost, 1)
                        pe.wait_ge(osqd, 3 * m + 1)
                        pe.matmul(SA[:], mean_v[:], osq[:], start=True, stop=True).then_inc(om, 1)
                turns(pe, turn)

            @block.scalar
            def _(act):
                act.preload_act_table_set(LN_EXP_SET)
                def turn(t, par, m, kv):
                    mp = 1 - par
                    for q in range(NB):
                        if t is not None:
                            bank = psum[q % 2]
                            if q == 0:
                                act.wait_ge(cur, t + 1)
                            if q != 2:
                                act.wait_ge(blocks, NB + NB * t + q + 1)
                            if q == 3:
                                act.activation(qa[par][:], bank[:], ACT.Identity, bias=now[par][:, 6:7]).then_inc(qa_ready, 1)
                            elif q != 2:
                                c = (0, 1, None, None, 2, 3, 4)[q]
                                if c >= 2 or not (isinstance(t, int) and t == 0):
                                    act.wait_ge(e_used, 5 * t + c - 1)
                                act.activation(e[c % 2][:], bank[:], ACT.Exp, bias=now[par][:, c:c + 1],
                                               scale=-1.0).then_inc(exps, 1)
                            if q == 0:
                                act.wait_ge(gates, t + 1)
                                act.activation(f1[:], f1[:], ACT.Ln).then_inc(lns, 1)
                                act.activation(f2[:], f2[:], ACT.Ln).then_inc(lns, 1)
                        if m is not None:
                            piece(q, m, mp)

                def decay(i, m, src):
                    act.wait_ge(dif, 8 * m + i + 1)
                    act.activation(src[:], src[:], ACT.Exp).then_inc(exd, 1)

                def piece(q, m, mp):
                    if q == 0:
                        act.wait_ge(proj_done, m + 1)
                        act.activation(e_b[:], bb[mp][:], ACT.Exp).then_inc(exd, 1)
                        decay(0, m, d_last)
                        decay(1, m, dd[0])
                    if q == 1:
                        act.wait_ge(mxs, m + 1)
                        act.activation(den[:], den[:], ACT.Exp).then_inc(sinke, 1)
                        for i, (u, n) in enumerate(units):
                            w = slice(P if n == 0 else 0, 2 * P)
                            act.activation(sc[:, u, n, w], sc[:, u, n, w], ACT.Exp, bias=negm[:, u, n:n + 1],
                                           accum_out=rs[:, u, n:n + 1]).then_inc(pex, 1)
                        decay(2, m, dd[1])
                        decay(3, m, dd[2])
                    if q == 2:
                        decay(4, m, dd[3])
                        decay(5, m, dd[0])
                    if q == 3:
                        act.wait_ge(ke_tr, m + 1)
                        act.activation(ke_t[:].rearrange("p c k -> p (c k)"), MX1[:], ACT.Copy).then_inc(ke_ev, 1)
                        decay(6, m, dd[1])
                        decay(7, m, dd[2])
                    if q in (3, 5):
                        for at in ((0, 1) if q == 3 else (2, 3)):
                            act.wait_ge(ptr, 4 * m + at + 1)
                            w = 4 if at < 3 else 2
                            act.activation(pt[:, 4 * at:4 * at + w].rearrange("p c t -> p (c t)"),
                                           (SA, SB_)[at % 2][:, 0:w * P], ACT.Copy).then_inc(pev, 1)
                    if q == 6:
                        act.wait_ge(ost, m + 1)
                        act.activation(osq[:], MX0[:], ACT.Square).then_inc(osqd, 1)
                        act.wait_ge(om, m + 1)
                        act.activation(rln[:], SA[:], ACT.Ln, bias=eps[:, 0:1]).then_inc(osqd, 1)
                        act.wait_ge(osqd, 3 * m + 2)
                        act.activation(rms[:], rln[:], ACT.Exp, scale=-0.5).then_inc(osqd, 1)
                turns(act, turn)

            PROJ, MIX = 11, 25

            @block.vector
            def _(dve):
                dve.sem_inc(fin, 1)
                order = Order(dve)

                def turn(t, par, m, kv):
                    mp = 1 - par
                    if t is not None:
                        st = Steps(dve, prj, t, PROJ)
                        if not (isinstance(t, int) and t == 0):
                            dve.wait_ge(proj_done, t)
                            dve.wait_ge(fin, t)
                        dve.tensor_scalar(now[par][:], g["pack"][:, t, :], 1.0, None, ALU.mult).then_inc(cur, 1)
                        dve.tensor_scalar(kcur[par][:], g["k_dup"][:, kv, :], 1.0, None, ALU.mult)
                        dve.tensor_scalar(vcur[par][:], g["v_kv"][:, :, bass.ds(kv * HD, HD)], 1.0, None,
                                          ALU.mult).then_inc(cur2, 1)
                        dve.wait_ge(cur, t + 1)
                    mst_ = Steps(dve, mst, m, MIX) if m is not None else None
                    for q in range(NB):
                        if t is not None:
                            proj(q, t, par, st)
                        if m is not None:
                            piece(q, m, mp, mst_)
                    if t is not None:
                        st.close()
                    if m is not None:
                        mst_.close()
                    order.last = None

                def proj(q, t, par, st):
                    bank = psum[q % 2]
                    order.wait()
                    if q == 2:
                        dve.wait_ge(blocks, NB + NB * t + q + 1)
                        dve.tensor_tensor(vh[par][:], bank[:].rearrange("p (c f) -> p c f", f=P),
                                          g["i_bias"][:, bass.ds(t * P, P)].unsqueeze(1).broadcast_to([P, NT, P]),
                                          ALU.add).then_inc(v_ready, 1)
                        order.ended(v_ready, t + 1)
                    if q in (2, 3):
                        return
                    no = (0, 1, None, None, 2, 3, 4)[q]
                    ex = e[no % 2]
                    dve.wait_ge(exps, 5 * t + no + 1)
                    first = dve.tensor_scalar(f1[:] if q == 4 else s[:], ex[:], BIG, 1.0, ALU.min, ALU.add)
                    if q == 0:
                        st.link(first)
                    else:
                        first.then_inc(e_used, 1)
                        dve.wait_ge(e_used, 5 * t + no + 1)
                    if q == 0:
                        st.link(dve.reciprocal(s[:], s[:]))
                        st.link(dve.tensor_scalar(s[:], s[:], now[par][:, 9:10], None, ALU.mult))
                        dve.scalar_tensor_tensor(kh[par][:], ex[:], BIG, s[:], ALU.min, ALU.mult).then_inc(e_used, 1)
                        st.did(dve.tensor_scalar(f1[:], s[:], now[par][:, 8:9], FLOOR, ALU.add, ALU.max))
                        st.sync()
                        st.link(dve.tensor_scalar(f2[:], f1[:], LN_CUT, 1.0 / LN_CUT, ALU.min, ALU.mult))
                        dve.tensor_scalar(f1[:], f1[:], LN_CUT, None, ALU.max).then_inc(gates, 1)
                        order.ended(gates, t + 1)
                    elif q == 1:
                        dve.wait_ge(lns, 2 * t + 2)
                        st.did(dve.tensor_tensor(f1[:], f1[:], f2[:], ALU.add))
                        st.link(dve.reciprocal(s[:], s[:]))
                        dve.scalar_tensor_tensor(qh[par][:], bank[:], now[par][:, 5:6], s[:], ALU.add,
                                                 ALU.mult).then_inc(q_ready, 1)
                        st.did(dve.tensor_tensor_scan(bb[par][:], g["chunk_keep"][:], f1[:], 0.0, ALU.mult, ALU.add))
                        order.ended(prj, st.base + st.n)
                    elif q == 4:
                        dve.tensor_scalar(gg[par][:], bank[:], now[par][:, 7:8], None, ALU.add).then_inc(og_ready, 1)
                        order.ended(og_ready, t + 1)
                    elif q == 5:
                        st.did(dve.reciprocal(ga[par][:], s[:]))
                        order.ended(prj, st.base + st.n)
                    elif q == 6:
                        st.link(dve.tensor_tensor(s[:], s[:], f1[:], ALU.mult))
                        st.link(dve.reciprocal(s[:], s[:]))
                        dve.tensor_tensor(gg[par][:], gg[par][:], s[:], ALU.mult).then_inc(proj_done, 1)
                        order.ended(proj_done, t + 1)

                def mulq(l, m, mp):
                    order.wait()
                    h = 64 >> l
                    dve.wait_ge(exd, 9 * m + l + 3)
                    if l >= 4:
                        dve.wait_ge(lev, 7 * m + l - 3)
                    dk, dq = halves(dd[l % 4], h)
                    rk, rq = halves(rr[l % 4], h)
                    kk, qq = halves(kh[mp], h)[0], halves(qh[mp], h)[1]
                    dve.tensor_tensor(rk, kk, dk, ALU.mult)
                    dve.tensor_tensor(rq, qq, dq, ALU.mult).then_inc(mul, 1)
                    order.ended(mul, 7 * m + l + 1)

                def add(l, m, mst_, n):
                    order.wait()
                    dve.wait_ge(lev, 7 * m + l + n)
                    bank = (AL0, AL1)[l // 2 % 2]
                    mst_.link(dve.tensor_tensor(
                        tmp[:, 0:n], bank[:, 0:n * 256].rearrange("p (l c t) -> p l c t", l=n, t=64),
                        g["level_mask"][:, l:l + n].unsqueeze(2).broadcast_to([P, n, NT, 64]), ALU.mult))
                    for i in range(l, l + n):
                        h = 64 >> i
                        av = aa[:].rearrange("p c (b i) -> p c b i", i=2 * h)[:, :, :, h:2 * h]
                        if i > l:
                            dve.wait_ge(acc, 7 * m + i)
                        dve.tensor_tensor(av, av, tmp[:, i - l].rearrange("p c (b i) -> p c b i", i=h),
                                          ALU.add).then_inc(acc, 1)
                    order.ended(acc, 7 * m + l + n)

                def piece(q, m, mp, k):
                    order.wait()
                    if q == 0:
                        dve.wait_ge(proj_done, m + 1)
                        dve.wait_ge(qk, m + 1)
                        dve.wait_ge(diag, m + 1)
                        dve.tensor_tensor(aa[:], MX0[:].rearrange("p (c t) -> p c t", t=P),
                                          ident[:].unsqueeze(1).broadcast_to([P, NT, P]), ALU.mult).then_inc(ke_r, 1)
                        for i, (u, n) in enumerate(units):
                            bank, c, w = score_at(u, n)
                            o = 2 * P - w
                            k.did(dve.tensor_tensor_reduce(sc[:, u, n, o:], bank[:, c:c + w], g["swa_mask"][:, o:],
                                                           ATT_SCALE, NEG, ALU.add, ALU.max, mx[:, u, n:n + 1]))
                        k.sync()
                        sink = now[mp][:, 10:12].unsqueeze(2).broadcast_to([P, 2, NT])
                        k.link(dve.tensor_tensor(mx[:], mx[:], sink, ALU.max))
                        k.did(dve.tensor_tensor(den[:], sink, mx[:], ALU.subtract))
                        dve.tensor_scalar(negm[:], mx[:], -1.0, None, ALU.mult).then_inc(mxs, 1)
                        order.ended(mxs, m + 1)
                    if q == 1:
                        dve.wait_ge(exd, 9 * m + 2)
                        dve.tensor_tensor(ke[:], kh[mp][:], d_last[:], ALU.mult).then_inc(ke_r, 1)
                        k.did(dve.tensor_tensor(qe[:], qh[mp][:], e_b[:], ALU.mult))
                        order.ended(k.sem, k.base + k.n)
                        mulq(0, m, mp)
                        order.wait()
                        dve.wait_ge(ke_r, 2 * m + 2)
                    if q == 2:
                        dve.wait_ge(pex, 8 * m + 8)
                        dve.wait_ge(sinke, m + 1)
                        k.link(dve.tensor_tensor(den[:], den[:], rs[:], ALU.add))
                        k.link(dve.reciprocal(den[:], den[:]))
                        k.did(dve.tensor_tensor(sc[:, :, 0, P:], sc[:, :, 0, P:],
                                                den[:, :, 0:1].broadcast_to([P, 2, P]), ALU.mult))
                        for u in range(2):
                            last = dve.tensor_tensor(sc[:, u, 1:], sc[:, u, 1:],
                                                     den[:, u, 1:].unsqueeze(2).broadcast_to([P, 3, 2 * P]), ALU.mult)
                        last.then_inc(pn, 1)
                        order.ended(pn, m + 1)
                        mulq(1, m, mp)
                        mulq(2, m, mp)
                    if q == 3:
                        mulq(3, m, mp)
                        mulq(4, m, mp)
                    if q == 4:
                        add(0, m, k, 2)
                        mulq(5, m, mp)
                        mulq(6, m, mp)
                        order.wait()
                        dve.wait_ge(st_mm, m + 1)
                        for c in range(3):
                            if c == 0:
                                last = dve.tensor_copy(state[:, 0], MX0[:, 0:P])
                            else:
                                last = dve.scalar_tensor_tensor(state[:, c], state[:, c - 1],
                                                                e_b[:, c * P + P - 1:c * P + P],
                                                                MX0[:, c * P:(c + 1) * P], ALU.mult, ALU.add)
                            last.then_inc(st_up, 1)
                            dve.wait_ge(st_up, 3 * m + c + 1)
                        add(2, m, k, 2)
                    if q == 5:
                        add(4, m, k, 2)
                        add(6, m, k, 1)
                    if q == 6:
                        dve.wait_ge(pvd, m + 1)
                        order.wait()
                        k.did(dve.tensor_tensor(tmp_att[:], MX1[:], ga[mp][:], ALU.mult))
                        dve.wait_ge(osqd, 3 * m + 3)
                        newton(dve, k, rms[:], rln[:], SA[:], eps[:, 0:1])
                        k.link(dve.scalar_tensor_tensor(oo[:], MX0[:], g["gn_hg"][:, 0:1], rms[:], ALU.mult, ALU.mult))
                        k.link(dve.tensor_tensor(oo[:], oo[:], gg[mp][:], ALU.mult))
                        dve.tensor_tensor(mix[:, m, :], oo[:], tmp_att[:], ALU.add).then_inc(fin, 1)
                turns(dve, turn)


def cross_phase(nc, psum, g):
    ident, eps, mix = g["ident"], g["eps"], g["mix"]
    R = g["routing"]
    NR = NG + NE
    with ExitStack() as ctx:
        def sb(name, shape, dt=F32):
            return ctx.enter_context(nc.sbuf_tensor(name, shape, dt))

        def sem(name):
            return ctx.enter_context(nc.semaphore(name))

        x_t, h_t = sb("x_t", [P, KC, SEQ]), sb("h_t", [P, KC, SEQ])
        h_rows = sb("h_rows", [P, NT, D])
        k_mem, v_mem = memory_views(h_rows)
        ring = sb("ring_c", [P, 4, KC, P])
        sq = sb("sq_c", [P, KC, SEQ])
        q_x = sb("q_x", [P, KC, SEQ])
        o_x = sb("o_x", [P, KC, SEQ])
        ln, r = sb("ln_c", [P, SEQ]), sb("r_c", [P, SEQ])
        sc = [sb(f"sc_c{i}", [P, NT, MEM]) for i in range(2)]
        pt = [sb(f"pt_c{i}", [P, MT, SEQ]) for i in range(2)]
        mx, rs, den = (sb(n, [P, XH, NT]) for n in ("mx_c", "rs_c", "den_c"))
        w_r = sb("w_r", [P, KC, NR])
        S = dense_sems(nc, ctx, "c")
        N = [norm_sems(nc, ctx, f"n{i}") for i in range(2)]
        w_r_landed = sem("w_r_landed")
        scores, maxed, exped, normed, turned, rows, outs, taken = (
            sem(n) for n in ("x_scores", "x_max", "x_exp", "x_probs", "x_turned", "x_rows_s", "x_out", "x_taken"))
        x_steps = sem("x_steps")
        logits_mm, rt, r_exp, counts, back, back_got, back_got_v = (
            sem(n) for n in ("logits", "route_steps", "route_exp", "places", "turned_back", "h_taken", "x_taken_back"))
        chosen, maxrow, maxrow_got = sem("chosen"), sem("places_max"), sem("longest_s")
        sq_summed = sem("squares_summed")
        consts, h_stored, x_back, kv_back = sem("route_consts"), sem("h_stored"), sem("x_back"), sem("kv_back")
        lg = sb("lg", [P, NT, NR])
        gp, geq = sb("gp", [P, NT, NG]), sb("geq", [P, NT, NG])
        g1, m1, m2, t1 = (sb(n, [P, NT]) for n in ("g1", "m1", "m2", "t1"))
        e_in, eq, oh1, oh2 = (sb(n, [P, NT, EPG]) for n in ("e_in", "eq", "oh1", "oh2"))
        prod = sb("prod", [P, NT, NG, EPG])
        sel1, sel2, both = (sb(n, [P, NT, NE]) for n in ("sel1", "sel2", "both"))
        rev = sb("rev", [P, EPG])
        e_base = sb("e_base", [P, NE])
        longest_f = sb("longest_f", [P, 1])
        place1, place2 = (q_x[:, 0, n:n + NT * NE].rearrange("p (t e) -> p t e", e=NE) for n in (0, NT * NE))
        in_pass = sb("in_pass", [P, NT, SEQ // SLOTS - 1])
        ROUTE_EXP = (3, 25)

        block = ctx.enter_context(nc.Block())

        def cols_of(w):
            v = w[0].rearrange("(k p) f -> p k f", p=P)
            return lambda e, n: v[:, :, bass.ds(e.snap(n * P), P)]

        @block.sync
        def _(sp):
            sp.dma_start(w_r[:], g["w_router"][0].rearrange("(k p) f -> p k f", p=P)).then_inc(w_r_landed, 16)
            for i, w in enumerate((g["w_out"], g["w_cq"], g["w_co"])):
                dense_load(sp, S, ring, cols_of(w), KC * i, KC)
            load_gate_up(sp, g, 0, 0, g["wgu0"])
            load_down(sp, g, 0, 0, g["wd0"])
            for t in range(NT):
                sp.wait_ge(back_got, NT + t + 1)
                sp.dma_start(g["h_dram"][t * P:(t + 1) * P, :], h_rows[:, t]).then_inc(h_stored, 16)
            sp.wait_ge(h_stored, 16 * NT)

        @block.gpsimd
        def _(pool):
            pool.iota(rev[:], [[-1, EPG]], base=EPG, channel_multiplier=0,
                      allow_small_or_imprecise_dtypes=True).then_inc(consts, 1)
            pool.iota(e_base[:], [[SLOTS, NE]], base=0, channel_multiplier=0,
                      allow_small_or_imprecise_dtypes=True).then_inc(consts, 1)
            pool.iota(g["token_id"][:], [[P, NT]], base=0, channel_multiplier=1,
                      allow_small_or_imprecise_dtypes=True).then_inc(consts, 1)
            for i in range(2):
                pool.wait_ge(N[i]["squared"], 1)
                for k in range(1, KC):
                    pool.wait_ge(N[i]["squared"], k + 1)
                    if k > 1:
                        pool.wait_ge(sq_summed, i * (KC - 1) + k - 1)
                    pool.tensor_tensor(sq[:, 0], sq[:, 0], sq[:, k], ALU.add).then_inc(sq_summed, 1)

        def head_scores(pe, h):
            if h >= 2:
                pe.wait_ge(exped, NT * (h - 1))
            for t in range(NT):
                bank = psum[2 * (h % 2) + t // 2]
                for c in range(2):
                    mm = pe.matmul(bank[:, t % 2 * MEM:(t % 2 + 1) * MEM], q_x[:, 2 * h + c, t * P:(t + 1) * P],
                                   k_mem[:, 2 * h + c], start=(c == 0), stop=(c == 1))
            mm.then_inc(scores, 1)

        @block.tensor
        def _(pe):
            def mean(i):
                pe.wait_ge(sq_summed, (i + 1) * (KC - 1))
                pe.matmul(psum[4][:], g["mean_d"][:], sq[:, 0], start=True, stop=True).then_inc(N[i]["mean"], 1)

            pe.sem_inc(S["mm"], 4)
            dense_mm(pe, S, ring, psum, mix, 0, KC, SEQ)
            mean(0)
            dense_mm(pe, S, ring, psum, h_t, KC, KC, SEQ, ready=N[0]["done"])
            pe.wait_ge(S["evac"], 4 + 2 * KC)
            pe.wait_ge(kv_back, 16)
            head_scores(pe, 0)
            for h in range(XH):
                if h + 1 < XH:
                    head_scores(pe, h + 1)
                pe.wait_ge(normed, h + 1)
                for m in range(MT):
                    if h:
                        pe.wait_ge(rows, MT * h - MT + m + 1)
                    for t in range(NT):
                        mm = pe.transpose(psum[4 + m][:, t * P:(t + 1) * P], sc[h % 2][:, t, m * P:(m + 1) * P],
                                          ident[:])
                    mm.then_inc(turned, 1)
                pe.wait_ge(rows, MT * (h + 1))
                for c in range(2):
                    if h:
                        pe.wait_ge(taken, 2 * h - 2 + c + 1)
                    for m in range(MT):
                        mm = pe.matmul(psum[6 + c][:], v_mem[:, m, (2 * h + c) * P:(2 * h + c + 1) * P],
                                       pt[h % 2][:, m], start=(m == 0), stop=(m == MT - 1))
                    mm.then_inc(outs, 1)
            pe.wait_ge(taken, 2 * XH)
            dense_mm(pe, S, ring, psum, o_x, 2 * KC, KC, SEQ)
            mean(1)
            pe.wait_ge(N[1]["done"], KC)
            pe.wait_ge(w_r_landed, 16)
            for t in range(NT):
                for k in range(KC):
                    mm = pe.matmul(psum[5][:, t * NR:(t + 1) * NR], h_t[:, k, t * P:(t + 1) * P], w_r[:, k],
                                   start=(k == 0), stop=(k == KC - 1))
            mm.then_inc(logits_mm, 1)
            pe.wait_ge(S["evac"], 4 + 3 * KC)
            for half in range(2):
                for t in range(NT):
                    for i, src in enumerate((h_t, x_t)):
                        no = half * NT + t
                        if no >= 2:
                            pe.wait_ge((back_got, back_got_v)[i], no - 1)
                        for k in range(4):
                            mm = pe.transpose(psum[2 * i + no % 2][:, k * P:(k + 1) * P],
                                              src[:, 4 * half + k, t * P:(t + 1) * P], ident[:])
                        mm.then_inc(back, 1)
            pe.wait_ge(chosen, 1)
            for t in range(NT):
                for u in range(t + 1):
                    mm = pe.matmul(psum[6][:, t * NE:(t + 1) * NE], (g["tri"] if u == t else g["ones"])[:], both[:, u],
                                   start=(u == 0), stop=(u == t))
            mm.then_inc(counts, 1)
            pe.wait_ge(maxrow, 1)
            pe.transpose(psum[7][0:1, 0:P], longest_f[:], ident[:]).then_inc(maxrow_got, 1)

        @block.scalar
        def _(act):
            act.preload_act_table_set(LN_EXP_SET)
            def norm(i, ready):
                n = N[i]
                for k in range(KC):
                    act.wait_ge(S["evac"], ready + k + 1)
                    act.activation(sq[:, k], x_t[:, k], ACT.Square).then_inc(n["squared"], 1)
                act.wait_ge(n["mean"], 1)
                act.activation(ln[:], psum[4][:], ACT.Ln, bias=eps[:, 0:1]).then_inc(n["squared"], 1)
                act.wait_ge(n["squared"], KC + 1)
                act.activation(r[:], ln[:], ACT.Exp, scale=-0.5).then_inc(n["rstd0"], 1)
            act.wait_ge(S["landed"][1], 16)
            act.dma_start(x_t[:], g["x_kept"]).then_inc(x_back, 16)
            act.dma_start(h_rows[:], g["kv_kept"]).then_inc(kv_back, 16)
            norm(0, 4)
            for h in range(XH):
                act.wait_ge(maxed, h + 1)
                if h >= 2:
                    act.wait_ge(turned, MT * (h - 1))
                for t in range(NT):
                    bank = psum[2 * (h % 2) + t // 2]
                    act.activation(sc[h % 2][:, t], bank[:, t % 2 * MEM:(t % 2 + 1) * MEM], ACT.Exp,
                                   bias=mx[:, h, t:t + 1], scale=X_SCALE,
                                   accum_out=rs[:, h, t:t + 1]).then_inc(exped, 1)
                for m in range(MT):
                    act.wait_ge(turned, MT * h + m + 1)
                    if h >= 2:
                        act.wait_ge(outs, 2 * (h - 1))
                    act.activation(pt[h % 2][:, m], psum[4 + m][:], ACT.Copy).then_inc(rows, 1)
            norm(1, 4 + 2 * KC)
            for no in range(2 * NT):
                act.wait_ge(back, 2 * no + 1)
                half, t = divmod(no, NT)
                act.activation(h_rows[:, t, 512 * half:512 * half + 512], psum[no % 2][:],
                               ACT.Copy).then_inc(back_got, 1)
                if no == 2:
                    act.wait_ge(rt, ROUTE_EXP[0])
                    act.activation(gp[:], gp[:], ACT.Exp).then_inc(r_exp, 1)
                if no == 5:
                    act.wait_ge(rt, ROUTE_EXP[1])
                    act.activation(t1[:], t1[:], ACT.Exp).then_inc(r_exp, 1)

        @block.vector
        def _(dve):
            dve.sem_inc(S["evac"], 4)
            dve.wait_ge(x_back, 16)

            def residual(n, q):
                return dve.tensor_tensor(x_t[:, n, :], x_t[:, n, :], psum[q][:], ALU.add)
            dense_out(dve, S, 0, KC, residual)
            norm_dve(dve, N[0], x_t, h_t, g["g_cross"], ln, r, psum[4], SEQ, eps)
            dense_out(dve, S, KC, KC, lambda n, q: dve.tensor_scalar(q_x[:, n, :], psum[q][:], 1.0, None, ALU.mult))
            st = Steps(dve, x_steps)

            def maxes(h):
                dve.wait_ge(scores, h + 1)
                for b in range(2):
                    st.did(dve.tensor_reduce(mx[:, h, 2 * b:2 * b + 2],
                                             psum[2 * (h % 2) + b][:].rearrange("p (t m) -> p t m", m=MEM), AX.X, ALU.max))
                st.sync()
                dve.tensor_scalar(mx[:, h], mx[:, h], -X_SCALE, None, ALU.mult).then_inc(maxed, 1)

            maxes(0)
            for h in range(XH):
                if h + 1 < XH:
                    maxes(h + 1)
                dve.wait_ge(exped, NT * (h + 1))
                st.link(dve.reciprocal(den[:, h], rs[:, h]))
                dve.tensor_tensor(sc[h % 2][:], sc[h % 2][:], den[:, h].unsqueeze(2).broadcast_to([P, NT, MEM]),
                                  ALU.mult).then_inc(normed, 1)
                for c in range(2):
                    dve.wait_ge(outs, 2 * h + c + 1)
                    dve.tensor_copy(o_x[:, 2 * h + c], psum[6 + c][:]).then_inc(taken, 1)
            dense_out(dve, S, 2 * KC, KC, residual)
            norm_dve(dve, N[1], x_t, h_t, g["g_ffn"], ln, r, psum[4], SEQ, eps)

            k = Steps(dve, rt)
            dve.wait_ge(logits_mm, 1)
            dve.wait_ge(consts, 2)
            k.link(dve.tensor_tensor(lg[:], psum[5][:, 0:NT * NR].rearrange("p (t f) -> p t f", f=NR),
                                     g["router_b"][:].unsqueeze(1).broadcast_to([P, NT, NR]), ALU.add))
            gl = lg[:, :, 0:NG]

            def bc(t, n):
                return t[:].unsqueeze(2).broadcast_to([P, NT, n])
            k.link(dve.tensor_reduce(g1[:], gl, AX.X, ALU.max))
            k.link(dve.tensor_tensor(gp[:], gl, bc(g1, NG), ALU.subtract))
            assert k.n == ROUTE_EXP[0]
            back_no = [0]

            def take_x(n):
                for _ in range(n):
                    no = back_no[0]
                    half, t = divmod(no, NT)
                    dve.wait_ge(back, 2 * no + 2)
                    dve.tensor_copy(g["x_rows"][:, t, 512 * half:512 * half + 512], psum[2 + no % 2][:]).then_inc(
                        back_got_v, 1)
                    back_no[0] += 1
            take_x(2)
            dve.wait_ge(r_exp, 1)
            k.link(dve.tensor_reduce(g1[:], gp[:], AX.X, ALU.add))
            k.link(dve.reciprocal(g1[:], g1[:]))
            k.link(dve.tensor_tensor(gp[:], gp[:], bc(g1, NG), ALU.mult))
            k.link(dve.tensor_reduce(g1[:], gp[:], AX.X, ALU.max))

            def first_max(one, values, top, n):
                k.link(dve.tensor_tensor(one, values, bc(top, n), ALU.is_equal))
                k.link(dve.tensor_tensor(one, one, rev[:, 0:n].unsqueeze(1).broadcast_to([P, NT, n]), ALU.mult))
                k.link(dve.tensor_reduce(t1[:], one, AX.X, ALU.max))
                k.link(dve.tensor_tensor(one, one, bc(t1, n), ALU.is_equal))
            first_max(geq[:], gp[:], g1, NG)
            grp = geq[:].unsqueeze(3).broadcast_to([P, NT, NG, EPG])
            k.link(dve.tensor_tensor(prod[:], lg[:, :, NG:].rearrange("p t (g e) -> p t g e", e=EPG), grp, ALU.mult))
            k.link(dve.tensor_reduce(e_in[:], prod[:].rearrange("p t g e -> p t e g"), AX.X, ALU.add))
            k.link(dve.tensor_reduce(m1[:], e_in[:], AX.X, ALU.max))
            first_max(oh1[:], e_in[:], m1, EPG)
            k.link(dve.scalar_tensor_tensor(eq[:], oh1[:], NEG, e_in[:], ALU.mult, ALU.add))
            k.link(dve.tensor_reduce(m2[:], eq[:], AX.X, ALU.max))
            first_max(oh2[:], eq[:], m2, EPG)
            k.link(dve.tensor_tensor(t1[:], m2[:], m1[:], ALU.subtract))
            assert k.n == ROUTE_EXP[1], k.n
            take_x(2)
            k.did(dve.tensor_tensor(sel1[:].rearrange("p t (g e) -> p t g e", e=EPG), grp,
                                    oh1[:].unsqueeze(2).broadcast_to([P, NT, NG, EPG]), ALU.mult))
            k.did(dve.tensor_tensor(sel2[:].rearrange("p t (g e) -> p t g e", e=EPG), grp,
                                    oh2[:].unsqueeze(2).broadcast_to([P, NT, NG, EPG]), ALU.mult))
            k.sync()
            dve.tensor_tensor(both[:], sel1[:], sel2[:], ALU.add).then_inc(chosen, 1)
            dve.wait_ge(chosen, 1)
            take_x(3)
            dve.wait_ge(r_exp, 2)
            k.link(dve.tensor_scalar(m1[:], t1[:], 1.0, None, ALU.add))
            k.link(dve.reciprocal(m1[:], m1[:]))
            k.did(dve.tensor_tensor(R["weight_1"][:], m1[:], g1[:], ALU.mult))
            k.link(dve.tensor_tensor(t1[:], t1[:], m1[:], ALU.mult))
            k.link(dve.tensor_tensor(R["weight_2"][:], t1[:], g1[:], ALU.mult))
            take_x(1)
            dve.wait_ge(counts, 1)
            places = psum[6][:, 0:NT * NE].rearrange("p (t e) -> p t e", e=NE)
            pr = prod[:].rearrange("p t g e -> p t (g e)")
            k.link(dve.tensor_tensor(pr, places, e_base[:].unsqueeze(1).broadcast_to([P, NT, NE]), ALU.add))
            for chosen_one, place, row in ((sel1, place1, R["row_1"]), (sel2, place2, R["row_2"])):
                k.did(dve.tensor_tensor(place[:], chosen_one[:], places, ALU.mult))
                k.link(dve.tensor_tensor(chosen_one[:], chosen_one[:], pr, ALU.mult))
                k.did(dve.tensor_reduce(m1[:], place[:], AX.X, ALU.add))
                k.link(dve.tensor_reduce(m2[:], chosen_one[:], AX.X, ALU.add))
                k.link(dve.tensor_tensor(in_pass[:], bc(m1, SEQ // SLOTS - 1), g["pass_first"][:], ALU.is_ge))
                k.link(dve.tensor_reduce(m1[:], in_pass[:], AX.X, ALU.add))
                k.link(dve.scalar_tensor_tensor(m2[:], m1[:], float((NE - 1) * SLOTS), m2[:], ALU.mult, ALU.add))
                k.link(dve.tensor_copy(row[:], m2[:]))
            far = 65536.0
            k.link(dve.scalar_tensor_tensor(pr, places, far, both[:], ALU.add, ALU.mult))
            k.link(dve.tensor_scalar(R["at_slot"][:], pr, -far, None, ALU.add))
            dve.tensor_reduce(longest_f[:], R["at_slot"][:], AX.XY, ALU.max).then_inc(maxrow, 1)
            dve.wait_ge(maxrow_got, 1)
            k.link(dve.tensor_reduce(t1[0:1, 0:1], psum[7][0:1, 0:P], AX.X, ALU.max))
            dve.tensor_copy(R["longest"][:], t1[0:1, 0:1]).then_inc(rt, 1)


def load_gate_up(eng, g, e, q, wgu):
    for k in (0, 4):
        half = g["w_gate_up"][0].rearrange("e (k p) f -> e p k f", p=P)[bass.ds(e, 1), :, k:k + 4, :]
        eng.dma_start(wgu[:, k:k + 4], half.rearrange("o p k f -> (o p) k f")).then_inc(
            g["weights_landed"]["gate_up"][q], 16)


def load_down(eng, g, e, q, wd):
    whole = g["w_down"][0].rearrange("e (k p) f -> e p k f", p=P)[bass.ds(e, 1)]
    eng.dma_start(wd[:], whole.rearrange("o p k f -> (o p) k f")).then_inc(g["weights_landed"]["down"][q], 16)


def expert_phase(nc, psum, g):
    ident, h_dram = g["ident"], g["h_dram"]
    R = g["routing"]
    y_dram = nc.dram_tensor("expert_out", (NE * SEQ, D), F32, kind="Internal").ap()
    FC = FF // P
    with ExitStack() as ctx:
        def sb(name, shape, dt=F32, c=ctx):
            return c.enter_context(nc.sbuf_tensor(name, shape, dt))

        def sem(name, c=ctx):
            return c.enter_context(nc.semaphore(name))

        wgu = [g["wgu0"], sb("wgu1", [P, KC, 2 * FF])]
        wd = [g["wd0"], sb("wd1", [P, FC, D])]
        sel = [sb(f"select{i}", [P, NT, SLOTS], F16) for i in range(2)]
        listed = [sb(f"listed{i}", [SLOTS, 1], U32) for i in range(2)]
        xr = [sb(f"xr{i}", [SLOTS, D]) for i in range(2)]
        xg = [sb(f"xg{i}", [P, KC, SLOTS]) for i in range(2)]
        ee = [sb(f"ee{i}", [P, FC, SLOTS]) for i in range(2)]
        hh = [sb(f"hh{i}", [P, FC, SLOTS]) for i in range(2)]
        yy = [sb(f"yy{i}", [SLOTS, D]) for i in range(2)]
        at_pass = sb("at_pass", [P, NT, NE])
        carrier = sb("carrier", [1, 2])

        def pick(dve, e, q, at):
            return dve.tensor_tensor(sel[q][:], g["slot_row"][:].unsqueeze(1).broadcast_to([P, NT, SLOTS]),
                                     at[:, :, bass.ds(e, 1)].broadcast_to([P, NT, SLOTS]), ALU.is_equal)

        def number(pe, q, bank):
            for t in range(NT):
                mm = pe.matmul(bank[0:SLOTS, 0:1], sel[q][:, t], g["token_id"][:, t:t + 1],
                               start=(t == 0), stop=(t == NT - 1))
            return mm

        def carry(pool):
            return pool.tensor_tensor(carrier[:, 1:2], carrier[:, 0:1], carrier[:, 0:1], ALU.add)

        def fetch(pool, q):
            return pool.indirect_dma_start(out=xr[q][:], out_offset=None, in_=h_dram[:, :],
                                           in_offset=bass.IndirectOffsetOnAxis(ap=listed[q][:, 0:1], axis=0))

        def turn_rows(pe, q, bank):
            for k in range(KC):
                mm = pe.transpose(bank[:, k * SLOTS:(k + 1) * SLOTS], xr[q][:, k * P:(k + 1) * P],
                                  ident[0:SLOTS, 0:SLOTS])
            return mm

        def gate_up(pe, q, bank, ks):
            for m in range(2 * FC):
                for k in ks:
                    mm = pe.matmul(bank[:, m * SLOTS:(m + 1) * SLOTS], wgu[q][:, k, m * P:(m + 1) * P], xg[q][:, k],
                                   start=(k == 0), stop=(k == KC - 1))
            return mm

        def down(pe, q, banks):
            for n in range(2):
                for f in range(FC):
                    mm = pe.matmul(banks[n][0:SLOTS, :], hh[q][:, f], wd[q][:, f, n * 512:(n + 1) * 512],
                                   start=(f == 0), stop=(f == FC - 1))
            return mm

        with ExitStack() as inner:
            def s2(name):
                return [sem(f"{name}{i}") for i in range(2)]
            gu, dn = g["weights_landed"]["gate_up"], g["weights_landed"]["down"]
            picked, numbered, copied, turned, gath_got, gu_mm, ex, used, hid, dn_mm, y_got = (
                sem(n) for n in ("picked", "numbered", "numbers_copied", "rows_turned", "rows_taken",
                                        "gate_up_mm", "gate_exp", "gate_steps", "hidden", "down_mm", "y_got"))
            pool_went = sem("pool_went")
            stored, fetched = s2("y_stored"), s2("rows_fetched")
            block = inner.enter_context(nc.Block())
            G, I, U, Y = psum[0], psum[1], (psum[2], psum[3]), ((psum[4], psum[5]), (psum[6], psum[7]))

            PAIRS = NE // 2

            def after(eng, s, n):
                if not isinstance(n, int) or n > 0:
                    eng.wait_ge(s, n)

            def over_experts(eng, turn):
                for i in (0, 1):
                    for q in range(2):
                        turn(i, q, 2 * i + q)
                with eng.Fori(2, PAIRS - 1) as i:
                    for q in range(2):
                        turn(i, q, 2 * i + q)
                for q in range(2):
                    turn(PAIRS - 1, q, NE - 2 + q)

            @block.sync
            def _(sp):
                for q in range(2):
                    sp.wait_ge(fetched[q], 16)
                load_gate_up(sp, g, 1, 1, wgu[1])
                load_down(sp, g, 1, 1, wd[1])
                sp.wait_ge(gu_mm, 1)
                load_gate_up(sp, g, 2, 0, wgu[0])

                def turn(i, q, e):
                    after(sp, gu_mm, e)
                    load_gate_up(sp, g, e + 1, 1 - q, wgu[1 - q])
                    after(sp, dn_mm, e - 1)
                    load_down(sp, g, e, q, wd[q])
                with sp.Fori(1, PAIRS - 1) as i:
                    for q in range(2):
                        turn(i, q, 2 * i + q)
                turn(PAIRS - 1, 0, NE - 2)
                sp.wait_ge(dn_mm, NE - 2)
                load_down(sp, g, NE - 1, 1, wd[1])

            @block.tensor
            def _(pe):
                def numbers(e, q, next_rows=None):
                    if next_rows is not None:
                        pe.wait_ge(fetched[1 - q], next_rows)
                    pe.wait_ge(picked, e + 1)
                    after(pe, copied, e)
                    number(pe, q, I).then_inc(numbered, 1)

                numbers(0, 0)
                numbers(1, 1)
                pe.wait_ge(fetched[0], 16)
                turn_rows(pe, 0, G).then_inc(turned, 1)

                def down_of(e, q, i):
                    pe.wait_ge(hid, e + 1)
                    pe.wait_ge(dn[q], 16 * i + 16)
                    after(pe, y_got, 2 * e - 2)
                    down(pe, q, Y[q]).then_inc(dn_mm, 1)

                def turn(i, q, e):
                    pe.wait_ge(gath_got, e + 1)
                    after(pe, hid, e - 1)
                    pe.wait_ge(gu[q], 32 * i + 32)
                    gate_up(pe, q, U[q], range(KC)).then_inc(gu_mm, 1)
                    ends = isinstance(e, int) and e >= NE - 2
                    rows_landed = 16 * i + 16 + 16 * q
                    if not ends:
                        numbers(e + 2, q, next_rows=rows_landed)
                    elif e == NE - 2:
                        pe.wait_ge(fetched[1], rows_landed)
                    if not (ends and q):
                        turn_rows(pe, 1 - q, G).then_inc(turned, 1)
                    if not (isinstance(e, int) and e == 0):
                        down_of(e - 1, 1 - q, i + q - 1)
                over_experts(pe, turn)
                down_of(NE - 1, 1, PAIRS - 1)

            @block.gpsimd
            def _(pool):
                pool.memset(carrier[:], 0.0).then_inc(pool_went, 1)

                def rows(i, q, e):
                    after(pool, copied, e + 1)
                    after(pool, turned, e - 1)
                    pool.wait_ge(pool_went, e + 1)
                    carry(pool).then_inc(pool_went, 1)
                    fetch(pool, q).then_inc(fetched[q], 16)
                over_experts(pool, rows)

            @block.scalar
            def _(act):
                act.preload_act_table_set(LN_EXP_SET)
                def take(e, q):
                    act.wait_ge(turned, e + 1)
                    after(act, gu_mm, e - 1)
                    act.activation(xg[q][:].rearrange("p k s -> p (k s)"), G[:], ACT.Copy).then_inc(gath_got, 1)

                def rows_out(e, q, i):
                    act.wait_ge(dn_mm, e + 1)
                    after(act, stored[q], 16 * i)
                    for n in range(2):
                        act.activation(yy[q][:, n * 512:(n + 1) * 512], Y[q][n][0:SLOTS, :], ACT.Copy).then_inc(y_got, 1)
                    dst = y_dram[bass.ds(act.snap(e * SLOTS) if not isinstance(e, int) else e * SLOTS, SLOTS), :]
                    act.wait_ge(y_got, 2 * e + 2)
                    act.dma_start(dst, yy[q][:]).then_inc(stored[q], 16)

                def turn(i, q, e):
                    act.wait_ge(gu_mm, e + 1)
                    after(act, hid, e - 1)
                    act.activation(ee[q][:].rearrange("p f s -> p (f s)"), U[q][:, 0:FC * SLOTS], ACT.Exp,
                                   scale=-1.0).then_inc(ex, 1)
                    if not (isinstance(e, int) and e == NE - 1):
                        take(e + 1, 1 - q)
                    if not (isinstance(e, int) and e == 0):
                        rows_out(e - 1, 1 - q, i + q - 1)
                take(0, 0)
                over_experts(act, turn)
                rows_out(NE - 1, 1, PAIRS - 1)
                for q in range(2):
                    act.wait_ge(stored[q], 16 * PAIRS)

            @block.vector
            def _(dve):
                def choose(e, q):
                    after(dve, numbered, e - 1)
                    pick(dve, e, q, R["at_slot"]).then_inc(picked, 1)

                def copy_numbers(i, q, e):
                    dve.wait_ge(numbered, e + 1)
                    after(dve, fetched[q], 16 * i)
                    dve.tensor_scalar(listed[q][:], I[0:SLOTS, 0:1], 1.0, None, ALU.mult).then_inc(copied, 1)

                def turn(i, q, e):
                    more = not (isinstance(e, int) and e >= NE - 2)
                    if more:
                        choose(e + 2, q)
                    after(dve, dn_mm, e - 1)
                    dve.wait_ge(ex, e + 1)
                    st = Steps(dve, used, e, 3)
                    gate, up = (U[q][:, c * 256:c * 256 + 256].rearrange("p (f s) -> p f s", s=SLOTS) for c in (0, 1))
                    st.link(dve.tensor_scalar(ee[q][:], ee[q][:], BIG, 1.0, ALU.min, ALU.add))
                    st.link(dve.reciprocal(ee[q][:], ee[q][:]))
                    st.link(dve.tensor_tensor(hh[q][:], gate, ee[q][:], ALU.mult))
                    st.close()
                    dve.tensor_tensor(hh[q][:], hh[q][:], up, ALU.mult).then_inc(hid, 1)
                    if more:
                        copy_numbers(i + 1, q, e + 2)
                choose(0, 0)
                choose(1, 1)
                copy_numbers(0, 0, 0)
                copy_numbers(0, 1, 1)
                over_experts(dve, turn)

        overflow_pass(nc, psum, g, locals())
    finish_phase(nc, psum, g, y_dram)


def overflow_pass(nc, psum, g, v):
    R = g["routing"]
    wgu, wd, xg, ee, hh, yy, listed = (v[n][0] for n in ("wgu", "wd", "xg", "ee", "hh", "yy", "listed"))
    at_pass, y_dram = v["at_pass"], v["y_dram"]
    pick, number, carry, fetch, turn_rows, gate_up, down = (v[n] for n in ("pick", "number", "carry", "fetch", "turn_rows", "gate_up",
                                                                    "down"))
    FC = FF // P
    PASSES = SEQ // SLOTS - 1
    with ExitStack() as ctx:
        picked, numbered, copied, turned, got, gu_mm, ex, hid, dn_mm, y_got, pool_went = (v[n] for n in (
            "picked", "numbered", "copied", "turned", "gath_got", "gu_mm", "ex", "hid", "dn_mm", "y_got", "pool_went"))
        fetched, stored, landed = v["fetched"][0], v["stored"][0], {n: w[0] for n, w in g["weights_landed"].items()}
        used = ctx.enter_context(nc.semaphore("over_steps"))
        HALF = NE // 2
        block = ctx.enter_context(nc.Block())
        G, I, U, Y = psum[0], psum[1], psum[2], (psum[4], psum[5])

        def turns(eng, turn):
            n = eng.value_load(R["longest"][0:1, 0:1], min_val=0, max_val=SEQ - 1)
            with eng.If(n >= SLOTS):
                with eng.Fori(0, PASSES) as p:
                    with eng.Fori(0, NE) as e:
                        turn(p, e, p * NE + e)

        @block.sync
        def _(sp):
            def turn(p, e, n):
                sp.wait_ge(stored, 16 * (n + HALF))
                load_gate_up(sp, g, e, 0, wgu)
                load_down(sp, g, e, 0, wd)
            turns(sp, turn)

        @block.tensor
        def _(pe):
            def turn(p, e, n):
                pe.wait_ge(picked, n + NE + 1)
                number(pe, 0, I).then_inc(numbered, 1)
                pe.wait_ge(fetched, 16 * (n + HALF) + 16)
                pe.matmul(I[:, 1:2], g["ident"][:], g["ident"][:, 0:1], start=True, stop=True)
                turn_rows(pe, 0, G).then_inc(turned, 1)
                pe.wait_ge(got, n + NE + 1)
                pe.wait_ge(landed["gate_up"], 32 * (n + HALF) + 32)
                gate_up(pe, 0, U, range(KC)).then_inc(gu_mm, 1)
                pe.wait_ge(hid, n + NE + 1)
                pe.wait_ge(landed["down"], 16 * (n + HALF) + 16)
                down(pe, 0, Y).then_inc(dn_mm, 1)
            turns(pe, turn)

        @block.gpsimd
        def _(pool):
            def turn(p, e, n):
                pool.wait_ge(copied, n + NE + 1)
                pool.wait_ge(pool_went, n + NE + 1)
                carry(pool).then_inc(pool_went, 1)
                fetch(pool, 0).then_inc(fetched, 16)
            turns(pool, turn)

        @block.scalar
        def _(act):
            act.preload_act_table_set(LN_EXP_SET)
            def turn(p, e, n):
                act.wait_ge(turned, n + NE + 1)
                act.activation(xg[:].rearrange("p k s -> p (k s)"), G[:], ACT.Copy).then_inc(got, 1)
                act.wait_ge(gu_mm, n + NE + 1)
                act.activation(ee[:].rearrange("p f s -> p (f s)"), U[:, 0:FC * SLOTS], ACT.Exp,
                               scale=-1.0).then_inc(ex, 1)
                act.wait_ge(dn_mm, n + NE + 1)
                for i in range(2):
                    act.activation(yy[:, i * 512:(i + 1) * 512], Y[i][0:SLOTS, :], ACT.Copy).then_inc(y_got, 1)
                dst = y_dram[bass.ds(act.snap((n + NE) * SLOTS), SLOTS), :]
                act.wait_ge(y_got, 2 * (n + NE) + 2)
                act.dma_start(dst, yy[:]).then_inc(stored, 16)
                act.wait_ge(stored, 16 * (n + HALF) + 16)
            turns(act, turn)

        @block.vector
        def _(dve):
            def turn(p, e, n):
                st = Steps(dve, used, n, 5)
                dve.wait_ge(stored, 16 * (n + HALF))
                st.link(dve.tensor_scalar(at_pass[:, 0], g["slot_row"][:, 0:NE], 0.0, None, ALU.mult))
                st.link(dve.tensor_tensor(at_pass[:], R["at_slot"][:], g["pass_first"][:, :, bass.ds(p, 1)].broadcast_to(
                    [P, NT, NE]), ALU.subtract))
                pick(dve, e, 0, at_pass).then_inc(picked, 1)
                dve.wait_ge(numbered, n + NE + 1)
                dve.tensor_scalar(listed[:], I[0:SLOTS, 0:1], 1.0, None, ALU.mult).then_inc(copied, 1)
                gate, up = (U[:, c * 256:c * 256 + 256].rearrange("p (f s) -> p f s", s=SLOTS) for c in (0, 1))
                dve.wait_ge(ex, n + NE + 1)
                st.link(dve.tensor_scalar(ee[:], ee[:], BIG, 1.0, ALU.min, ALU.add))
                st.link(dve.reciprocal(ee[:], ee[:]))
                st.link(dve.tensor_tensor(hh[:], gate, ee[:], ALU.mult))
                st.close()
                dve.tensor_tensor(hh[:], hh[:], up, ALU.mult).then_inc(hid, 1)
                dve.wait_ge(hid, n + NE + 1)
            turns(dve, turn)


def finish_phase(nc, psum, g, y_dram):
    x_rows, eps, R = g["x_rows"], g["eps"], g["routing"]
    with ExitStack() as ctx:
        def sb(name, shape, dt=F32):
            return ctx.enter_context(nc.sbuf_tensor(name, shape, dt))

        def sem(name):
            return ctx.enter_context(nc.semaphore(name))

        y1, y2 = sb("y1", [P, NT, D]), sb("y2", [P, NT, D])
        final_g = sb("final_g", [P, D])
        sqf = sb("sqf", [P, D])
        ss, lnf, rf, af = (sb(n, [P, NT]) for n in ("ss", "lnf", "rf", "af"))
        got = [sem(f"rows_back{t}") for t in range(NT)]
        g_landed, summed, sq_done, steps, done, stored = (
            sem(n) for n in ("g_landed", "summed", "sq_done", "fin_steps", "fin_done", "out_stored"))
        block = ctx.enter_context(nc.Block())

        @block.gpsimd
        def _(pool):
            def rows_of(table):
                for t in range(NT):
                    for y, row in ((y1, R["row_1"]), (y2, R["row_2"])):
                        pool.indirect_dma_start(out=y[:, t, :], out_offset=None, in_=table,
                                                in_offset=bass.IndirectOffsetOnAxis(ap=row[:, t:t + 1], axis=0)
                                                ).then_inc(got[t], 16)
            longest = pool.value_load(R["longest"][0:1, 0:1], min_val=0, max_val=SEQ - 1)
            with pool.If(longest >= SLOTS):
                rows_of(y_dram[:, :])
            with pool.Else():
                rows_of(y_dram[0:NE * SLOTS, :])

        @block.sync
        def _(sp):
            sp.dma_start(final_g[:], g["final_norm"].partition_broadcast(P)).then_inc(g_landed, 16)
            for t in range(NT):
                sp.wait_ge(done, t + 1)
                sp.dma_start(g["out"][0].rearrange("(n p) d -> n p d", p=P)[t], y2[:, t]).then_inc(stored, 16)
            sp.wait_ge(stored, 16 * NT)

        @block.vector
        def _(dve):
            k = Steps(dve, steps)
            dve.wait_ge(g_landed, 16)

            def total(t):
                dve.wait_ge(got[t], 32)
                k.did(dve.tensor_scalar(y1[:, t], y1[:, t], R["weight_1"][:, t:t + 1], None, ALU.mult))
                k.sync()
                k.link(dve.scalar_tensor_tensor(y1[:, t], y2[:, t], R["weight_2"][:, t:t + 1], y1[:, t], ALU.mult,
                                                ALU.add))
                dve.tensor_tensor(x_rows[:, t], x_rows[:, t], y1[:, t], ALU.add).then_inc(summed, 1)

            def scaled(t):
                dve.wait_ge(sq_done, 3 * t + 3)
                c = slice(t, t + 1)
                newton(dve, k, rf[:, c], af[:, c], ss[:, c], eps[:, 0:1])
                dve.scalar_tensor_tensor(y2[:, t], x_rows[:, t], rf[:, c], final_g[:], ALU.mult,
                                         ALU.mult).then_inc(done, 1)
            for t in range(NT):
                total(t)
                if t:
                    scaled(t - 1)
            scaled(NT - 1)

        @block.scalar
        def _(act):
            act.preload_act_table_set(LN_EXP_SET)
            for t in range(NT):
                c = slice(t, t + 1)
                act.wait_ge(summed, t + 1)
                if t:
                    act.wait_ge(sq_done, 3 * t)
                act.activation(sqf[:], x_rows[:, t], ACT.Square, scale=D ** -0.5, accum_out=ss[:, c]).then_inc(sq_done, 1)
                act.wait_ge(sq_done, 3 * t + 1)
                act.activation(lnf[:, c], ss[:, c], ACT.Ln, bias=eps[:, 0:1]).then_inc(sq_done, 1)
                act.wait_ge(sq_done, 3 * t + 2)
                act.activation(rf[:, c], lnf[:, c], ACT.Exp, scale=-0.5).then_inc(sq_done, 1)


_INS = ["x", "mem", "mix_norm", "w_in", "b_in", "attn_sinks", "hg_lb_logits", "hg_out_norm", "w_out", "cross_norm",
        "mem_norm", "w_cq", "w_ckv", "w_co", "ffn_norm", "w_router", "b_router", "w_gate_up", "w_down", "final_norm"]


def kernel(**inputs):
    import concourse.bacc as bacc
    from concourse.bass_utils import run_bass_kernel_spmd
    nc = bacc.Bacc("TRN2", target_bir_lowering=False, num_devices=1)
    arrays, args = {}, []
    for name in _INS:
        a = np.ascontiguousarray(inputs[name])
        arrays[f"in_{name}"] = a
        args.append(nc.dram_tensor(f"in_{name}", a.shape, mybir.dt.from_np(a.dtype), kind="ExternalInput").ap())
    out = nc.dram_tensor("out", (1, SEQ, D), F32, kind="ExternalOutput").ap()
    build_kernel(nc, *args, out)
    r = run_bass_kernel_spmd(nc, [arrays], core_ids=[0])
    return r.results[0]["out"]
```
